# Optimizing a Trainium2 kernel written in Bass

```python
import jax, jax.numpy as jnp
from jax import lax
import numpy as np
import math

D_MODEL = 1024
BATCH = 1
SEQ = 1024
DEPTH = 2

GRID_W = 64
CTX_LEN = 256
HEAD_DIM = 64
CONV_W = 256
CONV_GROUPS = 4
CONV_K = 3
RET_HEADS = 6
RET_W = RET_HEADS * HEAD_DIM
NA_HEADS = 6
NA_W = NA_HEADS * HEAD_DIM
MIX_W = CONV_W + RET_W + NA_W
RET_CHUNK = 128
WIN_H = 8
WIN_W = 16
ROPE_BASE = 10000.0
LN_EPS = 1e-5
DEEPNORM_ALPHA = (2 * DEPTH) ** 0.25
DEEPNORM_BETA = (8 * DEPTH) ** -0.25

PROJ_SPLITS = (RET_W, RET_W, NA_W, NA_W,
               RET_W, RET_W, NA_W, NA_W,
               CONV_W, CONV_W, CONV_W, CONV_W)
PROJ_W = sum(PROJ_SPLITS)
KV_W = 2 * RET_W + 2 * NA_W


F32 = jnp.float32

def split_cols(p, sizes):
    idx = np.cumsum(sizes)[:-1].tolist()
    return jnp.split(p, idx, axis=-1)

def to_heads(t, n_heads):
    b, l, _ = t.shape
    return t.reshape(b, l, n_heads, HEAD_DIM).transpose(0, 2, 1, 3)

def from_heads(t):
    b, h, l, d = t.shape
    return t.transpose(0, 2, 1, 3).reshape(b, l, h * d)

def layer_norm(x, g, b):
    xf = x.astype(F32)
    mu = jnp.mean(xf, axis=-1, keepdims=True)
    var = jnp.mean(jnp.square(xf - mu), axis=-1, keepdims=True)
    return ((xf - mu) * lax.rsqrt(var + LN_EPS) * g + b).astype(x.dtype)

def head_norm(o):
    of = o.astype(F32)
    mu = jnp.mean(of, axis=-1, keepdims=True)
    var = jnp.mean(jnp.square(of - mu), axis=-1, keepdims=True)
    return (of - mu) * lax.rsqrt(var + LN_EPS)

def axial_rope_angles(n):
    t = jnp.arange(n)
    row = (t // GRID_W).astype(F32)
    col = (t % GRID_W).astype(F32)
    nf = HEAD_DIM // 4
    inv = ROPE_BASE ** (-jnp.arange(nf, dtype=F32) / nf)
    return row[:, None] * inv, col[:, None] * inv

def rotate(xp, ang):
    a, b = jnp.split(xp, 2, axis=-1)
    cos, sin = jnp.cos(ang), jnp.sin(ang)
    return jnp.concatenate([a * cos - b * sin, a * sin + b * cos], axis=-1)

def apply_axial_rope(x, ang_r, ang_c):
    xr, xc = jnp.split(x, 2, axis=-1)
    return jnp.concatenate([rotate(xr, ang_r), rotate(xc, ang_c)], axis=-1).astype(x.dtype)

def short_conv_branch(h, bg, cg, z, w, b):
    u = cg * h
    up = jnp.pad(u, ((0, 0), (1, 1), (0, 0)))
    conv = up[:, :-2] * w[0] + up[:, 1:-1] * w[1] + up[:, 2:] * w[2] + b
    return bg * conv * jax.nn.silu(z)

def ret_final_state(k, v, lg):
    l = k.shape[2]
    w = jnp.exp((l - 1 - jnp.arange(l, dtype=F32))[None, :] * lg[:, None])
    return jnp.einsum('bhld,hl,bhle->bhde', k, w, v)

def chunk_retention(q, k, v, lg, s0, inclusive):
    b, h, l, dk = q.shape
    dv = v.shape[-1]
    c = min(RET_CHUNK, l)
    nc = l // c
    qc = q.reshape(b, h, nc, c, dk)
    kc = k.reshape(b, h, nc, c, dk)
    vc = v.reshape(b, h, nc, c, dv)
    i = jnp.arange(c, dtype=F32)
    diff = i[:, None] - i[None, :]
    mask = diff >= 0 if inclusive else diff > 0
    dmat = jnp.where(mask[None], jnp.exp(jnp.where(mask, diff, 0.0)[None] * lg[:, None, None]), 0.0)
    scores = jnp.einsum('bhnid,bhnjd->bhnij', qc, kc) * dmat[None, :, None]
    o_inner = jnp.einsum('bhnij,bhnje->bhnie', scores, vc)
    wk = jnp.exp((c - 1 - i)[None, :] * lg[:, None])
    u = jnp.einsum('bhnjd,hj,bhnje->bhnde', kc, wk, vc)
    g_chunk = jnp.exp(c * lg)[:, None, None]

    def step(s, u_n):
        return g_chunk * s + u_n, s

    _, s_prev = lax.scan(step, s0, jnp.moveaxis(u, 2, 0))
    s_prev = jnp.moveaxis(s_prev, 0, 2)
    wq = jnp.exp((i + 1)[None, :] * lg[:, None])
    o_cross = jnp.einsum('bhnid,hi,bhnde->bhnie', qc, wq, s_prev)
    return (o_inner + o_cross).reshape(b, h, l, dv)

def bidir_retention(q, k, v, lg_f, lg_b, s_f, s_b):
    fwd = chunk_retention(q, k, v, lg_f, s_f, True)
    bwd = chunk_retention(jnp.flip(q, 2), jnp.flip(k, 2), jnp.flip(v, 2), lg_b, s_b, False)
    return fwd + jnp.flip(bwd, 2)

def retention_branch(q, k, v, g, kc, vc, qc, gc, decay_logit, need_ctx):
    n = q.shape[1]
    kscale = HEAD_DIM ** -0.5
    ang_r, ang_c = axial_rope_angles(n)
    qh = apply_axial_rope(to_heads(q, RET_HEADS), ang_r, ang_c)
    kh = apply_axial_rope(to_heads(k, RET_HEADS), ang_r, ang_c) * kscale
    vh = to_heads(v, RET_HEADS)
    kch = to_heads(kc, RET_HEADS) * kscale
    vch = to_heads(vc, RET_HEADS)
    lg = jax.nn.log_sigmoid(decay_logit.astype(F32))
    lg_f, lg_b = lg[0], lg[1]
    s_f = ret_final_state(kch, vch, lg_f)
    s_b = ret_final_state(jnp.flip(kch, 2), jnp.flip(vch, 2), lg_b)
    o = bidir_retention(qh, kh, vh, lg_f, lg_b, s_f, s_b)
    y = from_heads(head_norm(o)) * jax.nn.silu(g)
    if not need_ctx:
        return y, None
    qch = to_heads(qc, RET_HEADS)
    zero = jnp.zeros_like(s_f)
    oc = bidir_retention(qch, kch, vch, lg_f, lg_b, zero, zero)
    yc = from_heads(head_norm(oc)) * jax.nn.silu(gc)
    return y, yc

def neighbourhood_branch(q, k, v, g, kc, vc, qc, gc, rpb, need_ctx):
    b, n, _ = q.shape
    rows = n // GRID_W
    win_h = min(WIN_H, rows)
    n_loc = win_h * WIN_W
    scale = HEAD_DIM ** -0.5

    def grid(t):
        return to_heads(t, NA_HEADS).reshape(b, NA_HEADS, rows, GRID_W, HEAD_DIM)

    qg, kg, vg = grid(q), grid(k), grid(v)
    kch, vch = to_heads(kc, NA_HEADS), to_heads(vc, NA_HEADS)
    r = np.arange(rows)
    row_start = np.clip(r - win_h // 2, 0, rows - win_h)
    d_row = row_start[:, None] + np.arange(win_h)[None, :] - r[:, None]
    cpos = np.arange(GRID_W)
    col_idx = np.clip(cpos - WIN_W // 2, 0, GRID_W - WIN_W)[:, None] + np.arange(WIN_W)[None, :]
    d_col = col_idx - cpos[:, None]

    def row_block(args):
        q_r, rs, dr = args
        k_band = lax.dynamic_slice_in_dim(kg, rs, win_h, axis=2)
        v_band = lax.dynamic_slice_in_dim(vg, rs, win_h, axis=2)
        k_win = k_band[:, :, :, col_idx]
        v_win = v_band[:, :, :, col_idx]
        s_loc = jnp.einsum('bhcd,bhrckd->bhcrk', q_r, k_win).astype(F32) * scale
        bias = rpb[:, dr[:, None, None] + (WIN_H - 1), d_col[None] + (WIN_W - 1)]
        s_loc = s_loc + bias.transpose(0, 2, 1, 3)[None].astype(F32)
        s_ctx = jnp.einsum('bhcd,bhjd->bhcj', q_r, kch).astype(F32) * scale
        p = jax.nn.softmax(jnp.concatenate([s_loc.reshape(b, NA_HEADS, GRID_W, n_loc), s_ctx], axis=-1), axis=-1)
        p_loc = p[..., :n_loc].reshape(b, NA_HEADS, GRID_W, win_h, WIN_W).astype(v.dtype)
        p_ctx = p[..., n_loc:].astype(v.dtype)
        return (jnp.einsum('bhcrk,bhrckd->bhcd', p_loc, v_win)
                + jnp.einsum('bhcj,bhjd->bhcd', p_ctx, vch))

    o = lax.map(row_block, (jnp.moveaxis(qg, 2, 0),
                            jnp.asarray(row_start, jnp.int32),
                            jnp.asarray(d_row, jnp.int32)))
    y = o.transpose(1, 0, 3, 2, 4).reshape(b, n, NA_W) * jax.nn.silu(g)
    if not need_ctx:
        return y, None
    qch = to_heads(qc, NA_HEADS)
    s = jnp.einsum('bhid,bhjd->bhij', qch, kch).astype(F32) * scale
    oc = jnp.einsum('bhij,bhjd->bhid', jax.nn.softmax(s, axis=-1).astype(vc.dtype), vch)
    yc = from_heads(oc) * jax.nn.silu(gc)
    return y, yc

def hybrid_layer(x, xc, c_act, cc_act, w_mod, b_mod, w_in, conv_w, conv_b,
                 ret_decay, na_rpb, w_out, ln_g, ln_b, need_ctx):
    shift, scale, gate = jnp.split(c_act @ w_mod + b_mod, 3, axis=-1)
    h = x * (1 + scale[:, None]) + shift[:, None]
    rk, rv, nk, nv, rq, rg, nq, ng, ch, cb, ccg, cz = split_cols(h @ w_in, PROJ_SPLITS)
    n_mod = 3 if need_ctx else 2
    mod_c = jnp.split(cc_act @ w_mod[:, :n_mod * D_MODEL] + b_mod[:n_mod * D_MODEL], n_mod)
    hc = xc * (1 + mod_c[1]) + mod_c[0]
    if need_ctx:
        pc = split_cols(hc @ w_in, PROJ_SPLITS)
    else:
        pc = split_cols(hc @ w_in[:, :KV_W], PROJ_SPLITS[:4]) + [None] * 8
    rkc, rvc, nkc, nvc, rqc, rgc, nqc, ngc, chc, cbc, ccc, czc = pc

    y_conv = short_conv_branch(ch, cb, ccg, cz, conv_w, conv_b)
    y_ret, yc_ret = retention_branch(rq, rk, rv, rg, rkc, rvc, rqc, rgc, ret_decay, need_ctx)
    y_na, yc_na = neighbourhood_branch(nq, nk, nv, ng, nkc, nvc, nqc, ngc, na_rpb, need_ctx)
    y = jnp.concatenate([y_conv, y_ret, y_na], axis=-1) @ w_out
    x_new = layer_norm(DEEPNORM_ALPHA * x + gate[:, None] * y, ln_g, ln_b)
    if not need_ctx:
        return x_new, None
    yc_conv = short_conv_branch(chc, cbc, ccc, czc, conv_w, conv_b)
    yc = jnp.concatenate([yc_conv, yc_ret, yc_na], axis=-1) @ w_out
    xc_new = layer_norm(DEEPNORM_ALPHA * xc + mod_c[2] * yc, ln_g, ln_b)
    return x_new, xc_new

def first_inputs(seed: int = 0) -> dict:
    key = jax.random.key(seed)
    ks = jax.random.split(key, 14)
    nrm = jax.random.normal
    x = nrm(ks[0], (BATCH, SEQ, D_MODEL), F32)
    c = nrm(ks[1], (BATCH, D_MODEL), F32)
    ctx = nrm(ks[2], (BATCH, CTX_LEN, D_MODEL), F32)
    c_ctx = nrm(ks[3], (D_MODEL,), F32)
    w_mod = nrm(ks[4], (DEPTH, D_MODEL, 3 * D_MODEL), F32) * (0.5 * D_MODEL ** -0.5)
    b_mod = 0.01 * nrm(ks[5], (DEPTH, 3 * D_MODEL), F32)
    w_in = nrm(ks[6], (DEPTH, D_MODEL, PROJ_W), F32) * (D_MODEL ** -0.5)
    conv_w = nrm(ks[7], (DEPTH, CONV_K, CONV_W), F32) * (CONV_K ** -0.5)
    conv_b = 0.01 * nrm(ks[8], (DEPTH, CONV_W), F32)
    gamma = 1.0 - 2.0 ** (-5.0 - np.arange(RET_HEADS))
    decay_init = np.log(gamma / (1.0 - gamma)).astype(np.float32)
    ret_decay = jnp.asarray(decay_init)[None, None, :] + 0.1 * nrm(ks[9], (DEPTH, 2, RET_HEADS), F32)
    na_rpb = 0.05 * nrm(ks[10], (DEPTH, NA_HEADS, 2 * WIN_H - 1, 2 * WIN_W - 1), F32)
    w_out = nrm(ks[11], (DEPTH, MIX_W, D_MODEL), F32) * (DEEPNORM_BETA * MIX_W ** -0.5)
    ln_g = 1.0 + 0.01 * nrm(ks[12], (DEPTH, D_MODEL), F32)
    ln_b = 0.01 * nrm(ks[13], (DEPTH, D_MODEL), F32)
    return {'x': x, 'c': c, 'ctx': ctx, 'c_ctx': c_ctx, 'w_mod': w_mod, 'b_mod': b_mod,
            'w_in': w_in, 'conv_w': conv_w, 'conv_b': conv_b, 'ret_decay': ret_decay,
            'na_rpb': na_rpb, 'w_out': w_out, 'ln_g': ln_g, 'ln_b': ln_b}

def first_block(x, c, ctx, c_ctx, w_mod, b_mod, w_in, conv_w, conv_b, ret_decay, na_rpb,
              w_out, ln_g, ln_b):
    c_act = jax.nn.silu(c)
    cc_act = jax.nn.silu(c_ctx)
    xc = ctx
    for l in range(DEPTH):
        x, xc = hybrid_layer(x, xc, c_act, cc_act, w_mod[l], b_mod[l], w_in[l], conv_w[l], conv_b[l],
                             ret_decay[l], na_rpb[l], w_out[l], ln_g[l], ln_b[l],
                             need_ctx=(l < DEPTH - 1))
    return x


DEPTH_2 = 1

POOL_WINDOWS = (2, 4, 8, 16)
POOL_GROUPS = len(POOL_WINDOWS)
POOL_WIDTH = D_MODEL // 2
POOL_GROUP_DIM = POOL_WIDTH // POOL_GROUPS
RNN_WIDTH = D_MODEL
RNN_HEADS = 16
RNN_HEAD_DIM = RNN_WIDTH // RNN_HEADS
RNN_CONV = 4
LRU_C = 8.0
D_FF = 3 * D_MODEL
FFN_CONV = 3
PLE_DIM = 256
N_BRANCH = 2
RMS_EPS = 1e-6
IN_POOL = POOL_WIDTH
IN_RNN_X = RNN_WIDTH
IN_RNN_G = RNN_WIDTH
IN_GATES = N_BRANCH * D_MODEL
IN_TOTAL = IN_POOL + IN_RNN_X + IN_RNN_G + IN_GATES


def rms_norm(x, g):
    xf = x.astype(jnp.float32)
    y = xf * lax.rsqrt(jnp.mean(xf * xf, axis=-1, keepdims=True) + RMS_EPS) * g.astype(jnp.float32)
    return y.astype(x.dtype)

def causal_dwconv(u, w, b):
    k_w = w.shape[0]
    s = u.shape[1]
    up = jnp.pad(u, ((0, 0), (k_w - 1, 0), (0, 0)))
    out = b + up[:, 0:s] * w[0]
    for k in range(1, k_w):
        out = out + up[:, k:k + s] * w[k]
    return out

def pool_mixer(u, pool_w, pool_scale):
    b, s, _ = u.shape
    uf = u.astype(jnp.float32)
    cs = jnp.pad(jnp.cumsum(uf, axis=1), ((0, 0), (1, 0), (0, 0)))
    t = jnp.arange(s, dtype=jnp.int32)
    outs = []
    for g, w in enumerate(POOL_WINDOWS):
        sl = cs[..., g * POOL_GROUP_DIM:(g + 1) * POOL_GROUP_DIM]
        prev = jnp.pad(sl, ((0, 0), (w - 1, 0), (0, 0)))[:, :s]
        count = jnp.minimum(t + 1, w).astype(jnp.float32)[None, :, None]
        outs.append((sl[:, 1:] - prev) / count)
    mean = jnp.concatenate(outs, axis=-1)
    d = (mean - uf).astype(u.dtype).reshape(b, s, POOL_GROUPS, POOL_GROUP_DIM)
    y = jnp.einsum('bsgc,gcd->bsgd', d, pool_w).reshape(b, s, POOL_WIDTH)
    return y * pool_scale

def rg_lru_branch(xb, gb, conv_w, conv_b, w_gates, b_gates, lru_lambda):
    b, s, _ = xb.shape
    xc = causal_dwconv(xb, conv_w, conv_b)
    xh = xc.reshape(b, s, RNN_HEADS, RNN_HEAD_DIM)
    gates = jnp.einsum('bshi,ghij->gbshj', xh, w_gates).reshape(2, b, s, RNN_WIDTH)
    gates = gates.astype(jnp.float32) + b_gates.astype(jnp.float32)[:, None, None, :]
    r = jax.nn.sigmoid(gates[0])
    i = jax.nn.sigmoid(gates[1])
    log_a = -LRU_C * r * jax.nn.softplus(-lru_lambda.astype(jnp.float32))
    a = jnp.exp(log_a)
    mult = jnp.sqrt(-jnp.expm1(2.0 * log_a))
    t0 = (jnp.arange(s) == 0)[None, :, None]
    mult = jnp.where(t0, 1.0, mult)
    u = mult * i * xc.astype(jnp.float32)

    def combine(left, right):
        a_l, h_l = left
        a_r, h_r = right
        return a_l * a_r, a_r * h_l + h_r

    _, h = lax.associative_scan(combine, (a, u), axis=1)
    return h.astype(xb.dtype) * jax.nn.gelu(gb)

def second_inputs(seed: int = 0) -> dict:
    key = jax.random.key(seed)
    ks = jax.random.split(key, 32)
    f32 = jnp.float32
    L = DEPTH_2

    def nrm(k, shape, fan_in):
        return jax.random.normal(k, shape, f32) * (fan_in ** -0.5)

    def gain(k, shape):
        return 1.0 + 0.05 * jax.random.normal(k, shape, f32)

    a_c = jax.random.uniform(ks[10], (L, RNN_WIDTH), f32, 0.9, 0.999)
    s_l = a_c ** (1.0 / LRU_C)
    lru_lambda = jnp.log(s_l) - jnp.log1p(-s_l)

    return {
        "x": jax.random.normal(ks[0], (BATCH, SEQ, D_MODEL), f32),
        "p": jax.random.normal(ks[1], (DEPTH_2, BATCH, SEQ, PLE_DIM), f32),
        "g_mix_pre": gain(ks[2], (L, D_MODEL)),
        "g_mix_post": gain(ks[3], (L, D_MODEL)),
        "w_in": nrm(ks[4], (L, D_MODEL, IN_TOTAL), D_MODEL),
        "pool_w": nrm(ks[5], (L, POOL_GROUPS, POOL_GROUP_DIM, POOL_GROUP_DIM), POOL_GROUP_DIM),
        "pool_scale": gain(ks[6], (L, POOL_WIDTH)),
        "w_pool_out": nrm(ks[7], (L, POOL_WIDTH, D_MODEL), POOL_WIDTH),
        "conv_w": nrm(ks[8], (L, RNN_CONV, RNN_WIDTH), RNN_CONV),
        "conv_b": 0.02 * jax.random.normal(ks[9], (L, RNN_WIDTH), f32),
        "w_rg_gates": nrm(ks[11], (L, 2, RNN_HEADS, RNN_HEAD_DIM, RNN_HEAD_DIM), RNN_HEAD_DIM),
        "b_rg_gates": 0.02 * jax.random.normal(ks[12], (L, 2, RNN_WIDTH), f32),
        "lru_lambda": lru_lambda,
        "w_rg_out": nrm(ks[13], (L, RNN_WIDTH, D_MODEL), RNN_WIDTH),
        "w_o": nrm(ks[14], (L, D_MODEL, D_MODEL), D_MODEL),
        "g_ffn_pre": gain(ks[15], (L, D_MODEL)),
        "g_ffn_post": gain(ks[16], (L, D_MODEL)),
        "w_up": nrm(ks[17], (L, D_MODEL, 2 * D_FF), D_MODEL),
        "ffn_conv_w": nrm(ks[18], (L, FFN_CONV, D_FF), FFN_CONV),
        "ffn_conv_b": 0.02 * jax.random.normal(ks[19], (L, D_FF), f32),
        "w_down": nrm(ks[20], (L, D_FF, D_MODEL), D_FF),
        "g_ple_gate": gain(ks[21], (L, D_MODEL)),
        "w_ple_gate": nrm(ks[22], (L, D_MODEL, D_MODEL), D_MODEL),
        "w_ple_proj": nrm(ks[23], (L, PLE_DIM, D_MODEL), PLE_DIM),
        "g_ple_post": gain(ks[24], (L, D_MODEL)),
    }

def second_block(x, p, g_mix_pre, g_mix_post, w_in, pool_w, pool_scale, w_pool_out,
              conv_w, conv_b, w_rg_gates, b_rg_gates, lru_lambda, w_rg_out, w_o,
              g_ffn_pre, g_ffn_post, w_up, ffn_conv_w, ffn_conv_b, w_down,
              g_ple_gate, w_ple_gate, w_ple_proj, g_ple_post):
    for l in range(DEPTH_2):
        h = rms_norm(x, g_mix_pre[l])
        z = h @ w_in[l]
        c0 = IN_POOL
        c1 = c0 + IN_RNN_X
        c2 = c1 + IN_RNN_G
        u_pool = z[..., :c0]
        u_rx = z[..., c0:c1]
        u_rg = z[..., c1:c2]
        gate_pool = jax.nn.sigmoid(z[..., c2:c2 + D_MODEL])
        gate_rnn = jax.nn.sigmoid(z[..., c2 + D_MODEL:])

        y_pool = pool_mixer(u_pool, pool_w[l], pool_scale[l]) @ w_pool_out[l]
        y_rnn = rg_lru_branch(u_rx, u_rg, conv_w[l], conv_b[l], w_rg_gates[l],
                              b_rg_gates[l], lru_lambda[l]) @ w_rg_out[l]
        merged = gate_pool * y_pool + gate_rnn * y_rnn
        x = x + rms_norm(merged @ w_o[l], g_mix_post[l])

        h = rms_norm(x, g_ffn_pre[l])
        up = h @ w_up[l]
        gate_h = causal_dwconv(up[..., :D_FF], ffn_conv_w[l], ffn_conv_b[l])
        hid = jax.nn.gelu(gate_h) * up[..., D_FF:]
        x = x + rms_norm(hid @ w_down[l], g_ffn_post[l])

        ple_gate = jax.nn.sigmoid(rms_norm(x, g_ple_gate[l]) @ w_ple_gate[l])
        ple = rms_norm(p[l].astype(x.dtype) @ w_ple_proj[l], g_ple_post[l])
        x = x + ple_gate * ple
    return x


def setup_inputs(seed=0):
    out = dict(first_inputs(seed))
    for name, value in second_inputs(seed + 1).items():
        if name != "x":
            out[name + "_2"] = value
    return out


def reference(
    x, c, ctx, c_ctx, w_mod, b_mod, w_in, conv_w, conv_b, ret_decay, na_rpb, w_out, ln_g, ln_b,
    p_2, g_mix_pre_2, g_mix_post_2, w_in_2, pool_w_2, pool_scale_2, w_pool_out_2, conv_w_2,
    conv_b_2, w_rg_gates_2, b_rg_gates_2, lru_lambda_2, w_rg_out_2, w_o_2, g_ffn_pre_2,
    g_ffn_post_2, w_up_2, ffn_conv_w_2, ffn_conv_b_2, w_down_2, g_ple_gate_2, w_ple_gate_2,
    w_ple_proj_2, g_ple_post_2,
):
    x = first_block(
        x, c, ctx, c_ctx, w_mod, b_mod, w_in, conv_w, conv_b, ret_decay, na_rpb, w_out, ln_g,
        ln_b,
    )
    return second_block(
        x, p_2, g_mix_pre_2, g_mix_post_2, w_in_2, pool_w_2, pool_scale_2, w_pool_out_2,
        conv_w_2, conv_b_2, w_rg_gates_2, b_rg_gates_2, lru_lambda_2, w_rg_out_2, w_o_2,
        g_ffn_pre_2, g_ffn_post_2, w_up_2, ffn_conv_w_2, ffn_conv_b_2, w_down_2, g_ple_gate_2,
        w_ple_gate_2, w_ple_proj_2, g_ple_post_2,
    )


_drawn_inputs = setup_inputs


def setup_inputs(seed=0):
    import zlib

    import numpy as np

    out = dict(_drawn_inputs(seed))
    spreads = {}
    factors = {'ctx': 3.256,
     'b_mod': 8.0,
     'conv_b': 51.425,
     'na_rpb': 64.0,
     'ln_g': 3.363,
     'b_rg_gates_2': 46.684,
     'ffn_conv_b_2': 5.164,
     'g_ple_gate_2': 22.815,
     'g_ple_post_2': 11.574,
     'ln_b': 7.24,
     'g_mix_pre_2': 3.297,
     'g_mix_post_2': 3.754,
     'pool_scale_2': 4.236,
     'conv_b_2': 2.668,
     'g_ffn_pre_2': 2.691,
     'g_ffn_post_2': 3.88}
    for name, (base, spread) in spreads.items():
        noise = np.random.default_rng([zlib.crc32(name.encode()), seed]).standard_normal(out[name].shape)
        drawn = base * np.exp(spread * noise) if base else spread * noise
        out[name] = __import__('jax').numpy.asarray(drawn.astype(out[name].dtype))
    for name, factor in factors.items():
        out[name] = (out[name] * factor).astype(out[name].dtype)
    return out
```

```python
from contextlib import ExitStack

import numpy as np
import concourse.bass as bass
from concourse import mybir

F32 = mybir.dt.float32
F32R = mybir.dt.float32r
ALU = mybir.AluOpType
ACT = mybir.ActivationFunctionType
AX = mybir.AxisListType

P = 128
D = 1024
KD = D // P
SEQ = 1024
CTX = 256
T1 = CTX + SEQ
NT = T1 // P
NC = CTX // P
HD = 64
PAIRS = 3
GRID_W, WIN_H, WIN_W = 64, 8, 16
ROWS = SEQ // GRID_W
QT = SEQ // P
KEYT = 5
LOC = KEYT * P
KEYS = LOC + CTX
ALPHA = 4.0 ** 0.25
LN_EPS, RMS_EPS = 1e-5, 1e-6
LRU_C = 8.0
MASKED = -1e30
FF_GROUPS, FF_CHUNKS = 3, 8

L_SLABS = 40
G_RET, G_NA, G_CONV, G_OUT = 0, 12, 24, 32
G_RNN = 2 * L_SLABS
G_RMIX = G_RNN + 16
G_POOL = G_RMIX + 16
G_PMIX = G_POOL + 4
G_WO = G_PMIX + 16
G_FFN = G_WO + 8
G_PLEP = G_FFN + FF_GROUPS * 24
G_PLEG = G_PLEP + 8
G_END = G_PLEG + 8
S8_GP = G_PMIX
S8_WO = S8_GP + 8
S8_PLEG = S8_WO + 8 + FF_GROUPS * 24
S8_END = S8_PLEG + 8

SPLITS = {}
_at = 0
for _name, _n in (("h0", 8), ("y0", 8), ("h1", 8), ("y1", 8), ("h2", 8), ("rnn", 8), ("pool", 4),
                  ("merged", 8), ("h3", 8), ("hid0", 8), ("hid1", 8), ("hid2", 8), ("p", 2), ("h4", 8)):
    SPLITS[_name] = _at
    _at += _n

VEC = {}
_at = 0
for _name, _n in (("bmod", 96), ("dec0", 18), ("dec1", 18), ("lam", 8), ("cols", 2),
                  ("convw0", 6), ("convb0", 2), ("lng0", 8), ("lnb0", 8),
                  ("convw1", 6), ("convb1", 2), ("lng1", 8), ("lnb1", 8),
                  ("g_mix_pre", 8), ("g_mix_post", 8), ("g_ffn_pre", 8), ("g_ffn_post", 8), ("g_ple_gate", 8),
                  ("g_ple_post", 8), ("pool_scale", 4), ("rconvw", 32), ("rconvb", 8), ("b_gates", 16),
                  ("fconvw", 72), ("fconvb", 24), ("eps", 2)):
    VEC[_name] = (_at, _n)
    _at += _n
NVEC = _at

TEMPS = {}
_at = 0
for _name in ("h0", "h1", "h2", "rnn", "h3", "hid0", "hid1", "hid2", "h4"):
    TEMPS[_name] = _at
    _at += 8


def o_groups(layer, pair):
    return 3 * pair if layer == 0 else 9 + 2 * pair


class Chain:

    def __init__(self, eng, sem):
        self.eng, self.sem, self.n, self.j, self.per, self.m = eng, sem, 0, None, 0, 0

    def count(self):
        return self.n if self.j is None else self.j * self.per + (self.n + self.m)

    def step(self, ins):
        ins.then_inc(self.sem, 1)
        if self.j is None:
            self.n += 1
        else:
            self.m += 1

    def link(self, ins):
        self.step(ins)
        self.eng.wait_ge(self.sem, self.count())

    def enter(self, j, per):
        self.j, self.per, self.m = j, per, 0

    def leave(self, turns):
        assert self.m == self.per, (self.m, self.per)
        self.n += turns * self.per
        self.j = None


def build_kernel(nc, xT, cT, modw, vecs, mats, ropes, rets, bias, s8, s4, s2, rgw, poolw, pooltab, pT, outT):
    V, A, T, G = nc.vector, nc.scalar, nc.tensor, nc.gpsimd
    with ExitStack() as ctx:
        arena = ctx.enter_context(nc.sbuf_tensor("arena", [P, 53208], F32))
        base = 229344 - 53208 * 4

        def at(name, word, shape, dt=F32):
            size = int(np.prod(shape[1:]))
            assert word + size <= 53208, name
            return nc.alloc_sbuf_tensor_at(name, shape, dt, offset=base + 4 * word)

        W_A, W_B, W_C = 0, 2 * KD * T1, 3 * KD * T1
        C_SIZE = 15232
        W_RING = W_C + C_SIZE
        W_SMALL = W_RING + 6 * 1024
        h_hi = at("h_hi", W_A, [P, KD, T1], F32R)
        h_lo = at("h_lo", W_A + KD * T1, [P, KD, T1], F32R)
        Y = at("Y", W_B, [P, KD, T1])
        QK = at("QK", W_C, [P, 6, T1])
        Vt = at("Vt", W_C + 6 * T1, [P, NT, 3 * P])
        W_CT = W_C + 6 * T1 + NT * 3 * P
        modring = at("modring", W_C, [P, 8, KD * P])
        cosT = at("cosT", W_CT, [P, SEQ])
        sinT = at("sinT", W_CT + SEQ, [P, SEQ])
        rope_tmp = at("rope_tmp", W_CT + 2 * SEQ, [P, SEQ])
        ret_const = at("ret_const", W_CT + 3 * SEQ, [P, 5, P])
        Dm = at("Dm", W_CT, [P, 6, P])
        WQ = at("WQ", W_CT + 768, [P, 2, 3, P])
        WK = at("WK", W_CT + 1536, [P, 2, 3 * P])
        dtmp = at("dtmp", W_CT + 2304, [P, 6, P])
        qw = at("qw", W_CT + 2304, [P, 2, 4 * P])
        kw = at("kw", W_B, [P, 2, NT, P])
        W_YNA = W_B + 5 * T1
        VT = at("VT", W_YNA, [P, 3, T1])
        ST = at("ST", W_YNA, [P, 2, NT, P])
        SD = at("SD", W_YNA + 2 * T1, [P, 2, 4 * P])
        hn_tmp = at("hn_tmp", W_B, [P, 2, T1])
        biasb = at("biasb", W_CT, [P, 2, 2, LOC])
        Sb = [at("Sb0", W_CT + 4 * LOC, [P, KEYS]), at("Sb1", W_B + KEYS, [P, KEYS])]
        PT = at("PT", W_B, [P, KEYS])
        QZ = at("QZ", W_B + 2 * KEYS, [P, 2, 2, P])
        OS = at("OS", W_B + 2 * KEYS + 512, [P, 2, P])
        ev = at("ev", W_C, [P, 4, T1])
        convu = at("convu", W_C + 4 * T1, [P, T1 + 4])
        convo = at("convo", W_C + 5 * T1 + 8, [P, T1 + 2])
        xin = at("xin", W_C, [P, KD, T1])
        stage = at("stage", W_C + 8 * T1, [P, 3, T1])
        g_hi = at("g_hi", 0, [P, KD, SEQ], F32R)
        g_lo = at("g_lo", 8192, [P, KD, SEQ], F32R)
        B2 = at("B2", 16384, [P, KD, SEQ])
        r_hi = at("r_hi", 24576, [P, KD, SEQ], F32R)
        r_lo = at("r_lo", 32768, [P, KD, SEQ], F32R)
        C2 = at("C2", 24576, [P, 2 * KD, SEQ])
        W_T2 = 40960
        T2 = at("T2", W_T2, [P, 4, SEQ])
        xb = at("xb", W_T2, [P, SEQ + 3])
        rgwt = at("rgwt", W_T2 + 1032, [P, 16, P])
        gpad = at("gpad", W_T2, [P, SEQ + 2])
        ffu = at("ffu", W_T2 + 1032, [P, SEQ])
        ffc = at("ffc", W_T2 + 2056, [P, SEQ])
        fft = at("fft", W_T2 + 3080, [P, SEQ])
        pu = at("pu", 28672, [P, SEQ + 16])
        pa = at("pa", 28672 + 1040, [P, SEQ + 16])
        pb = at("pb", 28672 + 2080, [P, SEQ + 16])
        p_hi = at("p_hi", W_T2, [P, 2, SEQ], F32R)
        p_lo = at("p_lo", W_T2 + 2048, [P, 2, SEQ], F32R)
        raw = [at(f"raw{s}", W_RING + 1024 * s, [P, KD * P]) for s in range(2)]
        w_hi = [at(f"w_hi{s}", W_RING + 2048 + 1024 * s, [P, KD * P], F32R) for s in range(2)]
        w_lo = [at(f"w_lo{s}", W_RING + 4096 + 1024 * s, [P, KD * P], F32R) for s in range(2)]
        cm = at("cm", W_SMALL, [P, 3, P])
        vec = at("vec", W_SMALL + 384, [P, NVEC])
        w = W_SMALL + 384 + (NVEC + 7) // 8 * 8
        cact = at("cact", w, [P, 3, KD * 2])
        mod = at("mod", w + 48, [P, 48, 2])
        lg = at("lg", w + 144, [P, 44])
        lru_c = at("lru_c", w + 192, [P, 2, 8])
        wk = at("wk", w + 208, [P, 12])
        gch = at("gch", w + 224, [P, 6])
        st = at("st", w + 232, [P, 2, 8])
        pool_zero = at("pool_zero", w + 248, [P, 8])
        lgt = at("lgt", W_CT, [P, 6, 44])
        ident, ones, blk = cm[:, 0, :], cm[:, 1, :], cm[:, 2, :]

        def vcol(name, i, n=1):
            o, size = VEC[name]
            assert i + n <= size
            return vec[:, o + i:o + i + n]

        ps = ctx.enter_context(nc.psum_tensor("ps", [P, 8 * 512], F32))
        BANK = 512

        x_saved = nc.dram_tensor("x_saved", [KD, P, T1], F32).ap()

        sems = {}

        def sem(name):
            sems[name] = ctx.enter_context(nc.semaphore(name))
            return sems[name]

        raw_loaded = [sem("raw_loaded0"), sem("raw_loaded1")]
        zero_set = sem("zero_set")
        hi_done, split_done = sem("hi_done"), sem("split_done")
        slab_done, evac_done = sem("slab_done"), sem("evac_done")
        const_in, x_in, mod_in = sem("const_in"), sem("x_in"), [sem(f"mod_in{i}") for i in range(8)]
        cact_ready, mod_used, mod_ready = sem("cact_ready"), sem("mod_used"), sem("mod_ready")
        sp_tmp, sp_hi, sp_lo = sem("sp_tmp"), sem("sp_hi"), sem("sp_lo")
        dve_step, act_step = sem("dve_step"), sem("act_step")
        tab_in, rot_ready, rope_done = sem("tab_in"), sem("rot_ready"), sem("rope_done")
        vt_ready, vt_used = sem("vt_ready"), sem("vt_used")
        kt_ready, kt_used = sem("kt_ready"), sem("kt_used")
        lg_ready, dtab, wtab = sem("lg_ready"), sem("dtab"), sem("wtab")
        u_ready, state_ready = sem("u_ready"), sem("state_ready")
        sc_ready, sd_ready, o_ready, o_used = sem("sc_ready"), sem("sd_ready"), sem("o_ready"), sem("o_used")
        hn_mean, hn_diff, hn_sq, hn_var, hn_std, hn_done = (sem("hn_mean"), sem("hn_diff"), sem("hn_sq"),
                                                            sem("hn_var"), sem("hn_std"), sem("hn_done"))
        bias_in = [sem("bias_in0"), sem("bias_in1")]
        qz_ready, s_ready, nm_ready = sem("qz_ready"), sem("s_ready"), sem("nm_ready")
        p_ready, pt_ready, pt_dve, pt_act = sem("p_ready"), sem("pt_ready"), sem("pt_dve"), sem("pt_act")
        rinv_ready, pv_ready, os_ready, ot_ready, ot_used = (sem("rinv_ready"), sem("pv_ready"), sem("os_ready"),
                                                             sem("ot_ready"), sem("ot_used"))
        qz_clear = sem("qz_clear")
        ev_used, conv_done = sem("ev_used"), sem("conv_done")
        xr_in, xs_out = sem("xr_in"), sem("xs_out")
        stat_sq, stat_used, stat_ready, std_ready, rs_ready = (sem("stat_sq"), sem("stat_used"), sem("stat_ready"),
                                                               sem("std_ready"), sem("rs_ready"))
        diff_ready, xn_ready = sem("diff_ready"), sem("xn_ready")
        rnn_xc, rnn_gates, rnn_act, rnn_m2, rnn_mult = (sem("rnn_xc"), sem("rnn_gates"), sem("rnn_act"),
                                                                  sem("rnn_m2"), sem("rnn_mult"))
        lam_ready, mix_used, pool_d, pool_ps = sem("lam_ready"), sem("mix_used"), sem("pool_d"), sem("pool_ps")
        ff_conv, ff_gelu, ff_used, acc_used, out_ready, out_done = (sem("ff_conv"), sem("ff_gelu"), sem("ff_used"),
                                                                    sem("acc_used"), sem("out_ready"), sem("out_done"))
        block = ctx.enter_context(nc.Block())

        RUNS = [(0, G_PMIX // 2, (s8, 0, 2), (s8, 1, 2), KD, KD),
                (G_PMIX, 8, (s8, S8_GP, 1), (s4, 0, 1), KD, 4),
                (G_WO, 40, (s8, S8_WO, 2), (s8, S8_WO + 1, 2), KD, KD),
                (G_PLEP, 4, (s2, 0, 2), (s2, 1, 2), 2, 2),
                (G_PLEG, 4, (s8, S8_PLEG, 2), (s8, S8_PLEG + 1, 2), KD, KD)]

        @block.sync
        def _(sp):
            def load(g, s, array, place, k):
                sp.dma_start(raw[s][:, :k * P], array[bass.ds(place, 1)].rearrange("a p n -> p (a n)"))\
                    .then_inc(raw_loaded[s], 16)

            for g0, pairs, a0, a1, k0, k1 in RUNS:
                if g0 == 0:
                    load(0, 0, s8, 0, KD)
                    load(1, 1, s8, 1, KD)
                lo = 1 if g0 == 0 else 0
                with sp.Fori(lo, pairs) as j:
                    for s, (array, place, step), k in ((0, a0, k0), (1, a1, k1)):
                        sp.wait_ge(split_done, j * 2 + (g0 + s - 1))
                        load(None, s, array, j * step + place, k)
            for n in range(KD):
                sp.wait_ge(out_ready, n + 1)
                sp.dma_start(outT[n], B2[:, n, :]).then_inc(out_done, 16)
            sp.wait_ge(out_done, 16 * KD)

        @block.gpsimd
        def _(pool):
            zero = pool_zero[:, 0:1]
            G.memset(zero, 0.0).then_inc(zero_set, 1)
            pool.wait_ge(zero_set, 1)

            def split(s, k, g):
                n = k * P
                G.tensor_tensor(w_hi[s][:, :n], raw[s][:, :n], zero.to_broadcast([P, n]), ALU.add).then_inc(hi_done, 1)
                pool.wait_ge(hi_done, g + 1)
                G.tensor_tensor(w_lo[s][:, :n], raw[s][:, :n], w_hi[s][:, :n].bitcast(F32), ALU.subtract)\
                    .then_inc(split_done, 1)

            for g0, pairs, a0, a1, k0, k1 in RUNS:
                if g0 == 0:
                    for s in range(2):
                        pool.wait_ge(raw_loaded[s], 16)
                        split(s, KD, s)
                lo = 1 if g0 == 0 else 0
                with pool.Fori(lo, pairs) as j:
                    for s, k in ((0, k0), (1, k1)):
                        g = j * 2 + (g0 + s)
                        pool.wait_ge(raw_loaded[s], j * 16 + (8 * g0 + 16))
                        pool.wait_ge(slab_done, g - 1)
                        split(s, k, g)

        FULL = [(0, 0, 512), (512, 512, 512), (1024, 1024, 256)]
        XONLY = [(CTX, 0, 512), (CTX + 512, 512, 512)]
        SEC = [(0, 0, 512), (512, 512, 512)]

        @block.tensor
        def _(pe):
            def slab(g, s, hi, lo, k_n, segs, slot, ready=None, first=False):
                pe.wait_ge(split_done, g + 1)
                if not first:
                    pe.wait_ge(evac_done, g - 1)
                o = s * slot * BANK
                for k in range(k_n):
                    if ready is not None:
                        pe.wait_ge(sp_lo, ready + k + 1)
                    kk = slice(k * P, (k + 1) * P)
                    for wt, xx, n in ((w_hi, hi, 0), (w_hi, lo, 1), (w_lo, hi, 2)):
                        for t0, c0, size in segs:
                            last = T.matmul(ps[:, o + c0:o + c0 + size], wt[s][:, kk], xx[:, k, t0:t0 + size],
                                            start=(k == 0 and n == 0), stop=(k == k_n - 1 and n == 2))
                last.then_inc(slab_done, 1)

            def gemm(g0, n, hi, lo, segs, slot, ready):
                for s in range(2):
                    slab(g0 + s, s, hi, lo, KD, segs, slot, ready if s == 0 else None, first=(g0 == 0))
                if n > 2:
                    with pe.Fori(1, n // 2) as j:
                        for s in range(2):
                            slab(j * 2 + (g0 + s), s, hi, lo, KD, segs, slot)

            pe.wait_ge(const_in, 48)
            pe.wait_ge(cact_ready, 1)
            with pe.Fori(0, 6) as j:
                for s in range(8):
                    pe.wait_ge(mod_in[s], j * 16 + 16)
                    for k in range(KD):
                        last = T.matmul(ps[:, bass.ds(j * 16 + (7 * BANK + 2 * s), 2)], modring[:, s, k * P:(k + 1) * P],
                                        cact[:, 2, 2 * k:2 * k + 2], start=(k == 0), stop=(k == KD - 1))
                    last.then_inc(mod_used, 1)

            for l in range(2):
                g0 = L_SLABS * l
                gemm(g0, 6, h_hi, h_lo, FULL, 3, SPLITS[f"h{l}"])
                pe.wait_ge(tab_in, 48 * (l + 1))
                with pe.Fori(0, 3) as j:
                    for s in range(2):
                        slab(j * 2 + (g0 + 6 + s), s, h_hi, h_lo, KD, FULL, 3)
                        pe.wait_ge(rope_done, j * 2 + (6 * l + s))
                        for half in range(2):
                            last = T.matmul(ps[:, (6 + half) * BANK:(7 + half) * BANK], ret_const[:, 0, :],
                                            QK[:, bass.ds(j * 2 + s, 1), CTX + 512 * half:CTX + 512 * (half + 1)],
                                            start=True, stop=True)
                        last.then_inc(rot_ready, 1)
                pe.wait_ge(rope_done, 6 * (l + 1))
                pe.wait_ge(evac_done, g0 + 12)
                groups = [(0, 4), (4, 4), (8, 2)]

                def transpose_values(first_unit):
                    u = first_unit
                    for c in range(3):
                        for n0, cnt in groups:
                            if u >= 2:
                                pe.wait_ge(vt_used, u - 1)
                            for t in range(cnt):
                                last = T.transpose(ps[:, (6 + u % 2) * BANK + t * P:(6 + u % 2) * BANK + (t + 1) * P],
                                                   VT[:, c, (n0 + t) * P:(n0 + t + 1) * P], ident)
                            last.then_inc(vt_ready, 1)
                            u += 1

                transpose_values(18 * l)
                pe.wait_ge(vt_used, 18 * l + 9)
                ku = 9 * l
                ogs = ([(0, 2)] if l == 0 else []) + [(2, 4), (6, 4)]
                for p in range(PAIRS):
                    for gi, (n0, cnt) in enumerate(groups):
                        u = ku + 3 * p + gi
                        if u >= 2:
                            pe.wait_ge(kt_used, u - 1)
                        if gi == 0 and (p or l):
                            pe.wait_ge(sd_ready, o_groups(l, p))
                        for t in range(cnt):
                            b = (6 + u % 2) * BANK + t * P
                            last = T.transpose(ps[:, b:b + P], QK[:, p, (n0 + t) * P:(n0 + t + 1) * P], ident)
                        last.then_inc(kt_ready, 1)
                    pe.wait_ge(kt_used, ku + 3 * p + 3)
                    if p or l:
                        pe.wait_ge(o_used, o_groups(l, p))
                    for d in range(2):
                        for n in range(NT):
                            if n == (NT - 1 if d == 0 else NC):
                                continue
                            b = 3 * d * BANK + n * P
                            last = T.matmul(ps[:, b:b + P], kw[:, d, n, :], Vt[:, n, p * P:(p + 1) * P],
                                            start=True, stop=True)
                    last.then_inc(u_ready, 1)
                    for i, (n0, cnt) in enumerate(ogs):
                        q = o_groups(l, p) + i
                        if i == 0:
                            pe.wait_ge(kt_used, ku + 3 * p + 3)
                        if q:
                            pe.wait_ge(sd_ready, q)
                        for a in range(2):
                            r = slice(HD * a, HD * (a + 1))
                            for t in range(cnt):
                                n = n0 + t
                                b = (6 + a) * BANK + t * P
                                last = T.matmul(ps[:, b:b + P], QK[r, p, n * P:(n + 1) * P],
                                                QK[r, 3 + p, n * P:(n + 1) * P], start=True, stop=True)
                        last.then_inc(sc_ready, 1)
                        pe.wait_ge(state_ready, 3 * l + p + 1)
                        pe.wait_ge(sd_ready, q + 1)
                        if q:
                            pe.wait_ge(o_used, q)
                        for t in range(cnt):
                            n = n0 + t
                            o = ps[:, t * P:(t + 1) * P]
                            terms = [d for d in range(2) if (d, n) not in ((0, 0), (1, NC - 1))]
                            for x, d in enumerate(terms):
                                T.matmul(o, ST[:, d, n, :], qw[:, d, t * P:(t + 1) * P], start=(x == 0), stop=False,
                                         skip_group_check=True)
                            for a in range(2):
                                last = T.matmul(ps[HD * a:HD * (a + 1), t * P:(t + 1) * P],
                                                Vt[:, n, p * P + HD * a:p * P + HD * (a + 1)],
                                                SD[:, a, t * P:(t + 1) * P], start=False, stop=(a == 1),
                                                skip_group_check=True)
                        last.then_inc(o_ready, 1)
                for p in range(PAIRS):
                    c = 3 * l + p
                    pe.wait_ge(o_used, o_groups(l, PAIRS))
                    if p:
                        pe.wait_ge(hn_diff, c)
                    for t0, c0, size in FULL:
                        last = T.matmul(ps[:, c0:c0 + size], blk, QK[:, 3 + p, t0:t0 + size], start=True, stop=True)
                    last.then_inc(hn_mean, 1)
                    pe.wait_ge(hn_sq, c + 1)
                    for t0, c0, size in FULL:
                        last = T.matmul(ps[:, 3 * BANK + c0:3 * BANK + c0 + size], blk, hn_tmp[:, 0, t0:t0 + size],
                                        start=True, stop=True)
                    last.then_inc(hn_var, 1)
                    pe.wait_ge(hn_std, c + 1)
                pe.wait_ge(hn_done, 3 * (l + 1))
                with pe.Fori(0, 4) as j:
                    for s in range(2):
                        slab(j * 2 + (g0 + G_NA + s), s, h_hi, h_lo, KD, FULL, 3)
                slab(g0 + G_NA + 8, 0, h_hi, h_lo, KD, FULL, 3)
                pe.wait_ge(evac_done, g0 + G_NA + 9)
                transpose_values(18 * l + 9)
                pe.wait_ge(vt_used, 18 * l + 18)
                slab(g0 + G_NA + 9, 1, h_hi, h_lo, KD, FULL, 3)
                for s in range(2):
                    slab(g0 + G_NA + 10 + s, s, h_hi, h_lo, KD, FULL, 3)
                pe.wait_ge(evac_done, g0 + G_NA + 12)
                tiles = QT + (NC if l == 0 else 0)
                per = 2 * tiles
                ub = 0 if l == 0 else 3 * 2 * (QT + NC)
                with pe.Fori(0, PAIRS) as j:
                    def scores(i):
                        u = j * per + (ub + i)
                        s, (t, a) = i % 2, divmod(i, 2)
                        pe.wait_ge(qz_ready, u + 1)
                        if i >= 2:
                            pe.wait_ge(p_ready, u - 1)
                        rows = QZ[:, t % 2, a, :]
                        o = 2 * s * BANK
                        if t < QT:
                            k0 = CTX + min(max(t - 2, 0), QT - KEYT) * P
                            T.matmul(ps[:, o:o + 512], rows, QK[:, bass.ds(j, 1), k0:k0 + 512], start=True, stop=True)
                            T.matmul(ps[:, o + 512:o + LOC], rows, QK[:, bass.ds(j, 1), k0 + 512:k0 + LOC],
                                     start=True, stop=True)
                        T.matmul(ps[:, o + LOC:o + KEYS], rows, QK[:, bass.ds(j, 1), 0:CTX], start=True, stop=True)\
                            .then_inc(s_ready, 1)

                    def apply(i):
                        u = j * per + (ub + i)
                        s, (t, a) = i % 2, divmod(i, 2)
                        first = 0 if t < QT else KEYT
                        pe.wait_ge(p_ready, u + 1)
                        lu = j * (2 * QT) + (6 * QT * l + min(i, 2 * QT))
                        if i:
                            pe.wait_ge(pt_dve, lu)
                            pe.wait_ge(pt_act, u)
                        for x in range(first, KEYT + NC):
                            last = T.transpose(ps[:, 4 * BANK + x * P:4 * BANK + (x + 1) * P], Sb[s][:, x * P:(x + 1) * P],
                                               ident)
                        last.then_inc(pt_ready, 1)
                        if t < QT:
                            pe.wait_ge(pt_dve, lu + 1)
                        pe.wait_ge(pt_act, u + 1)
                        if i:
                            pe.wait_ge(os_ready, u)
                        k0 = NC + min(max(t - 2, 0), QT - KEYT)
                        for x in range(first, KEYT + NC):
                            n = k0 + x if x < KEYT else x - KEYT
                            last = T.matmul(ps[:, 6 * BANK:6 * BANK + HD], PT[:, x * P:(x + 1) * P],
                                            Vt[:, n, bass.ds(j * P + HD * a, HD)], start=(x == first),
                                            stop=(x == KEYT + NC - 1))
                        last.then_inc(pv_ready, 1)

                    def turn(t):
                        n = j * tiles + (ub // 2 + t)
                        pe.wait_ge(os_ready, j * per + (ub + 2 * t + 2))
                        if t:
                            pe.wait_ge(ot_used, n)
                        T.transpose(ps[:, 7 * BANK:7 * BANK + P], OS[:, t % 2, :], ident).then_inc(ot_ready, 1)

                    scores(0)
                    for i in range(per):
                        if i + 1 < per:
                            scores(i + 1)
                        if i and i % 2 == 0:
                            turn(i // 2 - 1)
                        apply(i)
                    turn(tiles - 1)
                    pe.wait_ge(ot_used, j * tiles + (ub // 2 + tiles))
                with pe.Fori(0, 4) as j:
                    for s in range(2):
                        slab(j * 2 + (g0 + G_CONV + s), s, h_hi, h_lo, KD, FULL, 3)
                segs = FULL if l == 0 else XONLY
                gemm(g0 + G_OUT, 8, h_hi, h_lo, segs, 3, SPLITS[f"y{l}"])
                pe.wait_ge(evac_done, g0 + L_SLABS)
                for r in range(2):
                    for k in range(KD):
                        if r == 0:
                            pe.wait_ge(xn_ready, 8 * l + k + 1)
                        else:
                            pe.wait_ge(stat_sq, 8 * l + k + 1)
                        for t0, c0, size in segs:
                            last = T.matmul(ps[:, 3 * r * BANK + c0:3 * r * BANK + c0 + size], ones,
                                            Y[:, k, t0:t0 + size] if r == 0 else stage[:, k % 2, t0:t0 + size],
                                            start=(k == 0), stop=(k == KD - 1))
                        if r:
                            last.then_inc(stat_used, 1)
                    if r == 0:
                        last.then_inc(stat_ready, 1)
                pe.wait_ge(std_ready, l + 1)

            def sumsq(base_k):
                for k in range(KD):
                    sq = T2[:, k % 2, :] if base_k == 16 else C2[:, 8 + k, :]
                    pe.wait_ge(stat_sq, base_k + k + 1)
                    for t0, c0, size in SEC:
                        last = T.matmul(ps[:, 4 * BANK + c0:4 * BANK + c0 + size], ones, sq[:, t0:t0 + size],
                                        start=(k == 0), stop=(k == KD - 1))
                    last.then_inc(stat_used, 1)

            sumsq(16)
            for c in range(8):
                slab(G_RNN + 2 * c, 0, g_hi, g_lo, KD, SEC, 2, SPLITS["h2"] if c == 0 else None)
                slab(G_RNN + 2 * c + 1, 1, g_hi, g_lo, KD, SEC, 2)
                pe.wait_ge(tab_in, 112)
                pe.wait_ge(rnn_xc, c + 1)
                if c:
                    pe.wait_ge(rnn_act, c)
                for m in range(2):
                    for t0, c0, size in SEC:
                        last = T.matmul(ps[:, (4 + 2 * m) * BANK + c0:(4 + 2 * m) * BANK + c0 + size],
                                        rgwt[:, 8 * m + c, :], B2[:, 0, t0:t0 + size], start=True, stop=True)
                last.then_inc(rnn_gates, 1)
            for k in range(KD):
                slab(G_RMIX + 2 * k, 0, g_hi, g_lo, KD, SEC, 2)
                slab(G_RMIX + 2 * k + 1, 1, r_hi, r_lo, KD, SEC, 2, SPLITS["rnn"] if k == 0 else None)
            for c in range(5):
                if c < 4:
                    slab(G_POOL + c, c % 2, g_hi, g_lo, KD, SEC, 2)
                if c:
                    pe.wait_ge(pool_d, c)
                    if c > 1:
                        pe.wait_ge(sp_hi, SPLITS["pool"] + c - 1)
                    for t0, c0, size in SEC:
                        last = T.matmul(ps[:, 4 * BANK + c0:4 * BANK + c0 + size], C2[:, 15, (c - 1) * P:c * P],
                                        C2[:, 12, t0:t0 + size], start=True, stop=True)
                    last.then_inc(pool_ps, 1)
            for k in range(KD):
                slab(G_PMIX + 2 * k, 0, g_hi, g_lo, KD, SEC, 2)
                slab(G_PMIX + 2 * k + 1, 1, r_hi, r_lo, 4, SEC, 2, SPLITS["pool"] if k == 0 else None)
            gemm(G_WO, 8, g_hi, g_lo, SEC, 2, SPLITS["merged"])
            sumsq(24)
            sumsq(32)
            for f in range(FF_GROUPS):
                gf = G_FFN + 24 * f
                gemm(gf, 16, g_hi, g_lo, SEC, 2, SPLITS["h3"])
                gemm(gf + 16, 8, r_hi, r_lo, SEC, 2, SPLITS[f"hid{f}"])
            sumsq(40)
            sumsq(48)
            for n in range(8):
                slab(G_PLEP + n, n % 2, p_hi, p_lo, 2, SEC, 2, SPLITS["p"] if n == 0 else None)
            gemm(G_PLEG, 2, g_hi, g_lo, SEC, 2, SPLITS["h4"])
            sumsq(56)
            with pe.Fori(1, 4) as j:
                for s in range(2):
                    slab(j * 2 + (G_PLEG + s), s, g_hi, g_lo, KD, SEC, 2)

        def xcols(l):
            return slice(0 if l == 0 else CTX, T1)

        GROUPS = [(0, 4), (4, 4), (8, 2)]

        @block.scalar
        def _(act):
            own = Chain(act, act_step)

            def evac(g, dst, width, slot, func=ACT.Copy, scale=1.0):
                act.wait_ge(slab_done, g + 1)
                o = (g % 2) * slot * BANK
                A.activation(dst, ps[:, o:o + width], func, scale=scale).then_inc(evac_done, 1)

            def highs(name, n, src, hi, ready):
                for k in range(n):
                    ready(k)
                    A.activation(hi(k), src(k), ACT.Copy).then_inc(sp_hi, 1)

            def tmp_ready(name):
                return lambda k: act.wait_ge(sp_tmp, TEMPS[name] + k + 1)

            act.dma_start(cm[:], mats).then_inc(const_in, 16)
            act.dma_start(vec[:], vecs).then_inc(const_in, 16)
            act.dma_start(cact[:, 0, :], cT).then_inc(const_in, 16)
            for s in range(8):
                act.dma_start(modring[:, s, :], modw[s]).then_inc(mod_in[s], 16)
            act.dma_start(Y[:], xT.rearrange("k p t -> p k t")).then_inc(x_in, 16)
            act.wait_ge(const_in, 48)
            own.link(A.activation(cact[:, 1, :], cact[:, 0, :], ACT.Sigmoid))
            act.wait_ge(lg_ready, 1)
            A.activation(lgt[:, 2, :], lgt[:, 0, :], ACT.Exp, scale=-1.0).then_inc(lg_ready, 1)
            with act.Fori(1, 6) as j:
                for s in range(8):
                    act.wait_ge(mod_used, j * 8 + (s - 7))
                    act.dma_start(modring[:, s, :], modw[bass.ds(j * 8 + s, 1)].rearrange("a p n -> p (a n)"))\
                        .then_inc(mod_in[s], 16)
            highs("h0", KD, lambda k: stage[:, k % 3, :], lambda k: h_hi[:, k, :], tmp_ready("h0"))

            for l in range(2):
                g0 = L_SLABS * l
                act.wait_ge(sp_lo, SPLITS[f"h{l}"] + 8)
                act.dma_start(cosT[:], ropes[0]).then_inc(tab_in, 16)
                act.dma_start(sinT[:], ropes[1]).then_inc(tab_in, 16)
                act.dma_start(ret_const[:], rets).then_inc(tab_in, 16)
                if l:
                    act.wait_ge(xs_out, 16)
                for c in range(3):
                    evac(g0 + c, QK[:, c, :], T1, 3, scale=HD ** -0.5)
                for c in range(3):
                    evac(g0 + 3 + c, QK[:, 3 + c, :], T1, 3)
                for c in range(3):
                    evac(g0 + 6 + c, VT[:, c, :], T1, 3)
                for c in range(3):
                    evac(g0 + 9 + c, Y[:, 2 + c, :], T1, 3, ACT.Silu)

                def evac_values(first_unit):
                    for u in range(9):
                        c, (n0, cnt) = u // 3, GROUPS[u % 3]
                        uu = first_unit + u
                        act.wait_ge(vt_ready, uu + 1)
                        b = (6 + uu % 2) * BANK
                        A.activation(Vt[:, n0:n0 + cnt, c * P:(c + 1) * P],
                                     ps[:, b:b + cnt * P].rearrange("p (t f) -> p t f", f=P), ACT.Copy)\
                            .then_inc(vt_used, 1)

                act.wait_ge(dtab, l + 1)
                lgl = lg[:, 18 * l:18 * l + 18]
                A.activation(Dm[:], dtmp[:], ACT.Exp)
                for d in range(2):
                    for p in range(PAIRS):
                        c = 12 + 3 * d + p
                        A.activation(WQ[:, d, p, :], ret_const[:, 3 + d, :], ACT.Exp, scale=lgl[:, c:c + 1])
                own.link(A.activation(wk[:], wk[:], ACT.Exp))
                A.activation(gch[:], lgl[:, 12:18], ACT.Exp, scale=float(P)).then_inc(wtab, 1)
                evac_values(18 * l)
                ogs = ([(0, 2)] if l == 0 else []) + [(2, 4), (6, 4)]
                for p in range(PAIRS):
                    for i, (n0, cnt) in enumerate(ogs):
                        act.wait_ge(o_ready, o_groups(l, p) + i + 1)
                        A.activation(QK[:, 3 + p, n0 * P:(n0 + cnt) * P], ps[:, 0:cnt * P], ACT.Copy).then_inc(o_used, 1)
                for p in range(PAIRS):
                    c = 3 * l + p
                    act.wait_ge(hn_diff, c + 1)
                    if p:
                        act.wait_ge(hn_var, c)
                    A.activation(hn_tmp[:, 0, :], QK[:, 3 + p, :], ACT.Square).then_inc(hn_sq, 1)
                    act.wait_ge(hn_var, c + 1)
                    if p:
                        act.wait_ge(hn_done, c)
                    A.activation(hn_tmp[:, 1, :], ps[:, 3 * BANK:3 * BANK + T1], ACT.Sqrt, bias=vcol("eps", 0))\
                        .then_inc(hn_std, 1)
                ga = g0 + G_NA
                for c in range(3):
                    evac(ga + c, QK[:, c, :], T1, 3)
                for c in range(3):
                    evac(ga + 3 + c, QK[:, 3 + c, :], T1, 3, scale=HD ** -0.5)
                for c in range(3):
                    evac(ga + 6 + c, VT[:, c, :], T1, 3)
                evac_values(18 * l + 9)
                for c in range(3):
                    evac(ga + 9 + c, Y[:, 5 + c, :], T1, 3, ACT.Silu)
                tiles = QT + (NC if l == 0 else 0)
                per = 2 * tiles
                ub = 0 if l == 0 else 3 * 2 * (QT + NC)
                act.wait_ge(qz_clear, l + 1)
                with act.Fori(0, PAIRS) as j:
                    def load_bias(t):
                        act.dma_start(biasb[:, t % 2, :, :],
                                      bias[bass.ds(j * QT + (PAIRS * QT * l + t), 1)].rearrange("u p a n -> p (u a) n"))\
                            .then_inc(bias_in[t % 2], 16)

                    def query(i):
                        u = j * per + (ub + i)
                        t, a = divmod(i, 2)
                        c0 = CTX + t * P if t < QT else (t - QT) * P
                        if i >= 4:
                            act.wait_ge(s_ready, u - 3)
                        r = slice(HD * a, HD * (a + 1))
                        A.activation(QZ[r, t % 2, a, :], QK[r, bass.ds(j + 3, 1), c0:c0 + P], ACT.Copy)\
                            .then_inc(qz_ready, 1)

                    def exps(i):
                        u = j * per + (ub + i)
                        s, t = i % 2, i // 2
                        act.wait_ge(nm_ready, u + 1)
                        o = 2 * s * BANK
                        if t < QT:
                            A.activation(Sb[s][:, :LOC], Sb[s][:, :LOC], ACT.Exp, bias=st[:, s, 2:3],
                                         accum_out=st[:, s, 3:4])
                        A.activation(Sb[s][:, LOC:], ps[:, o + LOC:o + KEYS], ACT.Exp, bias=st[:, s, 2:3],
                                     accum_out=st[:, s, 4:5]).then_inc(p_ready, 1)

                    def rest(i):
                        u = j * per + (ub + i)
                        c0 = 512 if i < 2 * QT else LOC
                        act.wait_ge(pt_ready, u + 1)
                        A.activation(PT[:, c0:KEYS], ps[:, 4 * BANK + c0:4 * BANK + KEYS], ACT.Copy).then_inc(pt_act, 1)

                    def output(i):
                        u = j * per + (ub + i)
                        s, (t, a) = i % 2, divmod(i, 2)
                        act.wait_ge(rinv_ready, u + 1)
                        act.wait_ge(pv_ready, u + 1)
                        if t >= 2:
                            act.wait_ge(ot_ready, j * tiles + (ub // 2 + t - 1))
                        A.activation(OS[:, t % 2, HD * a:HD * (a + 1)], ps[:, 6 * BANK:6 * BANK + HD], ACT.Copy,
                                     scale=st[:, s, 6:7]).then_inc(os_ready, 1)

                    load_bias(0)
                    load_bias(1)
                    for i in range(3):
                        query(i)
                    exps(0)
                    for i in range(per):
                        rest(i)
                        if i + 3 < per:
                            query(i + 3)
                        if i + 1 < per:
                            exps(i + 1)
                            if i % 2 == 0 and i // 2 + 2 < QT:
                                load_bias(i // 2 + 2)
                        output(i)
                for c in range(2):
                    if c:
                        act.wait_ge(conv_done, 2 * l + 1)
                    for m in range(4):
                        evac(g0 + G_CONV + 4 * c + m, ev[:, m, :], T1, 3, ACT.Silu if m == 3 else ACT.Copy)
                act.wait_ge(conv_done, 2 * l + 2)
                act.dma_start(xin[:], (xT if l == 0 else x_saved).rearrange("k p t -> p k t")).then_inc(xr_in, 16)
                cs = xcols(l)
                highs(f"y{l}", KD, lambda k: Y[:, k, cs], lambda k: h_hi[:, k, cs], lambda k: None)
                for n in range(KD):
                    g = g0 + G_OUT + n
                    act.wait_ge(slab_done, g + 1)
                    if n >= 3:
                        act.wait_ge(xn_ready, 8 * l + n - 2)
                    o = (g % 2) * 3 * BANK
                    gate = 24 * l + 16 + n
                    if l == 0:
                        A.activation(stage[:, n % 3, :CTX], ps[:, o:o + CTX], ACT.Copy, scale=mod[:, gate, 1:2])
                        o += CTX
                    A.activation(stage[:, n % 3, CTX:], ps[:, o:o + SEQ], ACT.Copy, scale=mod[:, gate, 0:1])\
                        .then_inc(evac_done, 1)
                act.wait_ge(xn_ready, 8 * l + 8)
                for k in range(KD):
                    act.wait_ge(diff_ready, 8 * l + k + 1)
                    if k >= 2:
                        act.wait_ge(stat_used, 8 * l + k - 1)
                    A.activation(stage[:, k % 2, cs], Y[:, k, cs], ACT.Square).then_inc(stat_sq, 1)
                act.wait_ge(stat_used, 8 * l + 8)
                A.activation(stage[:, 2, cs], ps[:, 3 * BANK:3 * BANK + T1 - cs.start], ACT.Sqrt, bias=vcol("eps", 0))\
                    .then_inc(std_ready, 1)
                if l == 0:
                    highs("h1", KD, lambda k: xin[:, k, :], lambda k: h_hi[:, k, :], tmp_ready("h1"))
                    act.dma_start(x_saved.rearrange("k p t -> p k t"), Y[:]).then_inc(xs_out, 16)

            def squares(base_k, src, ready):
                for k in range(KD):
                    ready(k)
                    if base_k == 16:
                        if k >= 2:
                            act.wait_ge(stat_used, base_k + k - 1)
                        dst = T2[:, k % 2, :]
                    else:
                        dst = C2[:, 8 + k, :]
                    A.activation(dst, src(k), ACT.Square).then_inc(stat_sq, 1)

            def std(base_k, dst):
                act.wait_ge(stat_used, base_k + 8)
                A.activation(dst, ps[:, 4 * BANK:6 * BANK], ACT.Sqrt, bias=vcol("eps", 1)).then_inc(std_ready, 1)

            squares(16, lambda k: Y[:, k, CTX:], lambda k: act.wait_ge(xn_ready, 16 + k + 1))
            act.dma_start(x_saved.rearrange("k p t -> p k t")[:, :, CTX:], Y[:, :, CTX:]).then_inc(xs_out, 16)
            std(16, T2[:, 2, :])
            highs("h2", KD, lambda k: C2[:, 8 + k, :], lambda k: g_hi[:, k, :], tmp_ready("h2"))
            act.dma_start(rgwt[:], rgw.rearrange("g p n -> p g n")).then_inc(tab_in, 16)
            act.wait_ge(xs_out, 32)
            for c in range(8):
                if c:
                    act.wait_ge(rnn_xc, c)
                evac(G_RNN + 2 * c, xb[:, 3:], SEQ, 2)
                if c:
                    act.wait_ge(sp_tmp, TEMPS["rnn"] + c)
                evac(G_RNN + 2 * c + 1, B2[:, 1, :], SEQ, 2, ACT.Gelu_apprx_tanh)
                act.wait_ge(rnn_gates, c + 1)
                own.link(A.activation(B2[:, 2, :], ps[:, 4 * BANK:6 * BANK], ACT.Sigmoid, bias=vcol("b_gates", c)))
                A.activation(B2[:, 3, :], ps[:, 6 * BANK:8 * BANK], ACT.Sigmoid, bias=vcol("b_gates", 8 + c))\
                    .then_inc(rnn_act, 1)
                A.activation(B2[:, 4, :], B2[:, 2, :], ACT.Exp, scale=lru_c[:, 0, c:c + 1])
                A.activation(B2[:, 5, :], B2[:, 2, :], ACT.Tanh, scale=lru_c[:, 1, c:c + 1]).then_inc(rnn_m2, 1)
                act.wait_ge(rnn_mult, 2 * c + 1)
                A.activation(B2[:, 7, :], B2[:, 6, :], ACT.Sqrt).then_inc(rnn_mult, 1)
                act.wait_ge(sp_tmp, TEMPS["rnn"] + c + 1)
                A.activation(r_hi[:, c, :], B2[:, 6, :], ACT.Copy).then_inc(sp_hi, 1)

            def mix(g0, first):
                for n in range(KD):
                    if n + first >= 2:
                        act.wait_ge(mix_used, first + n - 1)
                    evac(g0 + 2 * n, T2[:, n % 2, :], SEQ, 2, ACT.Sigmoid)
                    evac(g0 + 2 * n + 1, T2[:, 2 + n % 2, :], SEQ, 2)

            mix(G_RMIX, 0)
            act.wait_ge(slab_done, G_POOL)
            act.dma_start(C2[:, 15, :4 * P], poolw.rearrange("g p n -> p g n")).then_inc(tab_in, 16)
            act.dma_start(C2[:, 14, :64], pooltab).then_inc(tab_in, 16)
            for c in range(5):
                if c < 4:
                    if c:
                        act.wait_ge(pool_d, c)
                    evac(G_POOL + c, pu[:, 16:], SEQ, 2)
                if c:
                    act.wait_ge(pool_ps, c)
                    if c > 1:
                        act.wait_ge(sp_lo, SPLITS["pool"] + c - 1)
                    own.link(A.activation(C2[:, 13, :], ps[:, 4 * BANK:6 * BANK], ACT.Copy, scale=vcol("pool_scale", c - 1)))
                    A.activation(r_hi[:, c - 1, :], C2[:, 13, :], ACT.Copy).then_inc(sp_hi, 1)
            mix(G_PMIX, 8)
            act.wait_ge(slab_done, G_WO)
            highs("merged", KD, lambda k: B2[:, k, :], lambda k: g_hi[:, k, :],
                  lambda k: act.wait_ge(mix_used, 8 + k + 1))
            act.wait_ge(sp_lo, SPLITS["merged"] + 8)
            act.dma_start(B2[:], x_saved.rearrange("k p t -> p k t")[:, :, CTX:]).then_inc(xr_in, 16)
            for n in range(KD):
                evac(G_WO + n, C2[:, n, :], SEQ, 2)
            squares(24, lambda k: C2[:, k, :], lambda k: act.wait_ge(evac_done, G_WO + k + 1))
            std(24, T2[:, 2, :])
            act.wait_ge(stat_used, 32)
            squares(32, lambda k: B2[:, k, :], lambda k: act.wait_ge(xn_ready, 24 + k + 1))
            act.dma_start(x_saved.rearrange("k p t -> p k t")[:, :, CTX:], B2[:]).then_inc(xs_out, 16)
            std(32, T2[:, 2, :])
            act.wait_ge(slab_done, G_FFN)
            highs("h3", KD, lambda k: C2[:, k, :], lambda k: g_hi[:, k, :], tmp_ready("h3"))
            act.wait_ge(xs_out, 48)
            for f in range(FF_GROUPS):
                gf = G_FFN + 24 * f
                for c in range(FF_CHUNKS):
                    cc = FF_CHUNKS * f + c
                    if cc:
                        act.wait_ge(ff_conv, cc)
                    evac(gf + 2 * c, gpad[:, 2:], SEQ, 2)
                    act.wait_ge(ff_conv, cc + 1)
                    A.activation(ffc[:], ffc[:], ACT.Gelu_apprx_tanh, bias=vcol("fconvb", cc)).then_inc(ff_gelu, 1)
                    if c == 0 and f > 1:
                        act.wait_ge(acc_used, 8 * (f - 1))
                    evac(gf + 2 * c + 1, ffu[:], SEQ, 2)
                    act.wait_ge(sp_tmp, TEMPS[f"hid{f}"] + c + 1)
                    A.activation(r_hi[:, c, :], fft[:], ACT.Copy).then_inc(sp_hi, 1)
                for n in range(KD):
                    if f == 0:
                        evac(gf + 16 + n, B2[:, n, :], SEQ, 2)
                    else:
                        if n >= 2:
                            act.wait_ge(acc_used, 8 * (f - 1) + n - 1)
                        evac(gf + 16 + n, (ffu, fft)[n % 2][:], SEQ, 2)
            act.dma_start(C2[:, 0:8, :], x_saved.rearrange("k p t -> p k t")[:, :, CTX:]).then_inc(xr_in, 16)
            squares(40, lambda k: B2[:, k, :], lambda k: act.wait_ge(acc_used, 8 + k + 1))
            std(40, T2[:, 2, :])
            squares(48, lambda k: B2[:, k, :], lambda k: act.wait_ge(xn_ready, 32 + k + 1))
            act.dma_start(C2[:, 0:2, :], pT.rearrange("k p t -> p k t")).then_inc(tab_in, 16)
            std(48, C2[:, 7, :])
            act.wait_ge(tab_in, 160)
            highs("p", 2, lambda k: C2[:, k, :], lambda k: p_hi[:, k, :], lambda k: None)
            highs("h4", KD, lambda k: C2[:, 8 + k, :], lambda k: g_hi[:, k, :], tmp_ready("h4"))
            for n in range(KD):
                evac(G_PLEP + n, C2[:, n, :], SEQ, 2)
            act.wait_ge(sp_lo, SPLITS["h4"] + 8)
            squares(56, lambda k: C2[:, k, :], lambda k: act.wait_ge(evac_done, G_PLEP + k + 1))
            for n in range(KD):
                if n == 2:
                    std(56, T2[:, 2, :])
                if n >= 2:
                    act.wait_ge(out_ready, n - 1)
                evac(G_PLEG + n, T2[:, n % 2, :], SEQ, 2, ACT.Sigmoid)

        @block.vector
        def _(dve):
            own = Chain(dve, dve_step)

            def lows(name, n, src, hi, lo, make=None):
                for k in range(n + 1):
                    if 3 <= k < n and make is not None:
                        dve.wait_ge(sp_lo, SPLITS[name] + k - 2)
                    if k < n and make is not None:
                        make(k).then_inc(sp_tmp, 1)
                    if k:
                        dve.wait_ge(sp_hi, SPLITS[name] + k)
                        V.tensor_tensor(lo(k - 1), src(k - 1), hi(k - 1).bitcast(F32), ALU.subtract).then_inc(sp_lo, 1)

            dve.wait_ge(const_in, 48)
            lin = vec[:, VEC["dec0"][0]:VEC["dec0"][0] + 44]
            own.link(V.scalar_tensor_tensor(lgt[:, 0, :], lin, -1.0, lin, ALU.mult, ALU.max))
            V.tensor_scalar(lgt[:, 1, :], lin, 0.0, None, ALU.min).then_inc(lg_ready, 1)
            dve.wait_ge(act_step, 1)
            V.tensor_tensor(cact[:, 2, :], cact[:, 0, :], cact[:, 1, :], ALU.mult).then_inc(cact_ready, 1)
            dve.wait_ge(lg_ready, 2)
            own.link(V.tensor_scalar(lgt[:, 3, :], lgt[:, 2, :], 2.0, None, ALU.add))
            own.link(V.reciprocal(lgt[:, 3, :], lgt[:, 3, :]))
            own.link(V.tensor_tensor(lgt[:, 2, :], lgt[:, 2, :], lgt[:, 3, :], ALU.mult))
            own.link(V.tensor_tensor(lgt[:, 3, :], lgt[:, 2, :], lgt[:, 2, :], ALU.mult))
            own.link(V.tensor_scalar(lgt[:, 4, :], lgt[:, 3, :], 1.0 / 17, 1.0 / 15, ALU.mult, ALU.add))
            for m in (13, 11, 9, 7, 5, 3, 1):
                own.link(V.tensor_tensor(lgt[:, 4, :], lgt[:, 4, :], lgt[:, 3, :], ALU.mult))
                own.link(V.tensor_scalar(lgt[:, 4, :], lgt[:, 4, :], 1.0 / m, None, ALU.add))
            own.link(V.scalar_tensor_tensor(lgt[:, 5, :], lgt[:, 2, :], -2.0, lgt[:, 4, :], ALU.mult, ALU.mult))
            own.link(V.tensor_tensor(lg[:], lgt[:, 5, :], lgt[:, 1, :], ALU.add))
            own.link(V.tensor_scalar(lru_c[:, 0, :], lg[:, 36:44], LRU_C, None, ALU.mult))
            own.link(V.tensor_scalar(lru_c[:, 1, :], lg[:, 36:44], -LRU_C, None, ALU.mult))
            dve.wait_ge(mod_used, 48)
            own.link(V.tensor_tensor(mod[:].rearrange("p a b -> p (a b)"), ps[:, 7 * BANK:7 * BANK + 96],
                                     vcol("bmod", 0, 96), ALU.add))
            for l in range(2):
                own.link(V.tensor_scalar(mod[:, 24 * l + 8:24 * l + 16, :], mod[:, 24 * l + 8:24 * l + 16, :], 1.0, None,
                                         ALU.add))
            dve.wait_ge(x_in, 16)

            def modulated(l, dst, src, k):
                a, b = 24 * l + 8 + k, 24 * l + k
                V.tensor_scalar(dst[:, :CTX], src[:, :CTX], mod[:, a, 1:2], mod[:, b, 1:2], ALU.mult, ALU.add)
                return V.tensor_scalar(dst[:, CTX:], src[:, CTX:], mod[:, a, 0:1], mod[:, b, 0:1], ALU.mult, ALU.add)

            lows("h0", KD, lambda k: stage[:, k % 3, :], lambda k: h_hi[:, k, :], lambda k: h_lo[:, k, :],
                 lambda k: modulated(0, stage[:, k % 3, :], Y[:, k, :], k))

            for l in range(2):
                g0 = L_SLABS * l
                lgl = lg[:, 18 * l:18 * l + 18]
                dve.wait_ge(tab_in, 48 * (l + 1))
                for c in range(6):
                    x = QK[:, c, CTX:]
                    dve.wait_ge(rot_ready, 6 * l + c + 1)
                    dve.wait_ge(rope_done, 6 * l + c)
                    own.link(V.tensor_tensor(rope_tmp[:], ps[:, 6 * BANK:8 * BANK], sinT[:], ALU.mult))
                    own.link(V.tensor_tensor(x, x, cosT[:], ALU.mult))
                    V.tensor_tensor(x, x, rope_tmp[:], ALU.add).then_inc(rope_done, 1)
                dve.wait_ge(rope_done, 6 * l + 6)
                for h in range(6):
                    own.link(V.tensor_scalar(dtmp[:, h, :], ret_const[:, 1, :], lgl[:, h:h + 1], None, ALU.mult))
                    own.link(V.scalar_tensor_tensor(dtmp[:, h, :], ret_const[:, 2, :], lgl[:, 6 + h:7 + h], dtmp[:, h, :],
                                                    ALU.mult, ALU.add))
                V.tensor_scalar(wk[:, 0:6], lgl[:, 0:6], vcol("cols", 0), None, ALU.mult)
                V.tensor_scalar(wk[:, 6:12], lgl[:, 6:12], vcol("cols", 1), None, ALU.mult).then_inc(dtab, 1)
                dve.wait_ge(vt_ready, 18 * l + 9)
                own.link(V.memset(ST[:], 0.0))
                dve.wait_ge(wtab, l + 1)
                ogs = ([(0, 2)] if l == 0 else []) + [(2, 4), (6, 4)]
                if l:
                    dve.wait_ge(xs_out, 16)
                for p in range(PAIRS):
                    for gi, (n0, cnt) in enumerate(GROUPS):
                        u = 9 * l + 3 * p + gi
                        dve.wait_ge(kt_ready, u + 1)
                        if gi == 0 and 3 * l + p:
                            dve.wait_ge(u_ready, 3 * l + p)
                        b = (6 + u % 2) * BANK
                        src = ps[:, b:b + cnt * P].rearrange("p (t f) -> p t f", f=P)
                        for d in range(2):
                            for a in range(2):
                                c = 6 * d + 2 * p + a
                                last = V.tensor_scalar(kw[:, d, n0:n0 + cnt, HD * a:HD * (a + 1)],
                                                       src[:, :, HD * a:HD * (a + 1)], wk[:, c:c + 1], None, ALU.mult)
                        last.then_inc(kt_used, 1)
                    dve.wait_ge(u_ready, 3 * l + p + 1)
                    if o_groups(l, p):
                        dve.wait_ge(o_ready, o_groups(l, p))
                    steps = {0: [(1, None, 0)] + [(n + 1, n, n) for n in range(1, NT - 1)],
                             1: [(0, None, 1), (NT - 1, 0, 0)] + [(n - 1, n, n) for n in range(NT - 1, NC, -1)]}
                    for x in range(9):
                        for d in range(2):
                            dst, prev, un = steps[d][x]
                            for a in range(2):
                                r = slice(HD * a, HD * (a + 1))
                                uu = ps[r, 3 * d * BANK + un * P + HD * a:3 * d * BANK + un * P + HD * (a + 1)]
                                if prev is None:
                                    ins = V.tensor_copy(ST[r, d, dst, r], uu)
                                else:
                                    ins = V.scalar_tensor_tensor(ST[r, d, dst, r], ST[r, d, prev, r],
                                                                 gch[r, 3 * d + p:3 * d + p + 1], uu, ALU.mult, ALU.add)
                                if x == 8 and d == 1 and a == 1:
                                    ins.then_inc(state_ready, 1)
                                else:
                                    ins.then_inc(dve_step, 1)
                                    own.n += 1
                        if x < 8:
                            dve.wait_ge(dve_step, own.n)
                    for i, (n0, cnt) in enumerate(ogs):
                        q = o_groups(l, p) + i
                        if q:
                            dve.wait_ge(o_ready, q)
                        qs = QK[:, 3 + p, n0 * P:(n0 + cnt) * P].rearrange("p (t f) -> p t f", f=P)
                        for d in range(2):
                            V.tensor_tensor(qw[:, d, :cnt * P].rearrange("p (t f) -> p t f", f=P), qs,
                                            WQ[:, d, p, :].unsqueeze(1).to_broadcast([P, cnt, P]), ALU.mult)
                        dve.wait_ge(sc_ready, q + 1)
                        for a in range(2):
                            b = (6 + a) * BANK
                            last = V.tensor_tensor(SD[:, a, :cnt * P].rearrange("p (t f) -> p t f", f=P),
                                                   ps[:, b:b + cnt * P].rearrange("p (t f) -> p t f", f=P),
                                                   Dm[:, 2 * p + a, :].unsqueeze(1).to_broadcast([P, cnt, P]), ALU.mult)
                        last.then_inc(sd_ready, 1)
                for p in range(PAIRS):
                    c = 3 * l + p
                    o = QK[:, 3 + p, :]
                    dve.wait_ge(hn_mean, c + 1)
                    V.tensor_tensor(o, o, ps[:, 0:T1], ALU.subtract).then_inc(hn_diff, 1)
                    dve.wait_ge(hn_std, c + 1)
                    own.link(V.reciprocal(hn_tmp[:, 1, :], hn_tmp[:, 1, :]))
                    own.link(V.tensor_tensor(o, o, hn_tmp[:, 1, :], ALU.mult))
                    V.tensor_tensor(Y[:, 2 + p, :], Y[:, 2 + p, :], o, ALU.mult).then_inc(hn_done, 1)
                V.memset(QZ[:], 0.0).then_inc(qz_clear, 1)
                tiles = QT + (NC if l == 0 else 0)
                per = 2 * tiles
                ub = 0 if l == 0 else 3 * 2 * (QT + NC)
                locals_ = 2 * QT
                steps_per = locals_ * 3 + (per - locals_)
                with dve.Fori(0, PAIRS) as j:
                    own.enter(j, steps_per)

                    def maxima(i):
                        u = j * per + (ub + i)
                        s, (t, a) = i % 2, divmod(i, 2)
                        o = 2 * s * BANK
                        dve.wait_ge(s_ready, u + 1)
                        if i >= 2:
                            dve.wait_ge(p_ready, u - 1)
                        if t < QT:
                            dve.wait_ge(bias_in[t % 2], j * (16 * QT // 2) + (16 * (3 * QT // 2 * l + t // 2 + 1)))
                        if i >= 2:
                            dve.wait_ge(pt_ready, u - 1)
                        if t < QT:
                            own.step(V.reduce_max(st[:, s, 0:1], ps[:, o + LOC:o + KEYS], AX.X))
                            own.link(V.tensor_tensor_reduce(out=Sb[s][:, :LOC], in0=ps[:, o:o + LOC],
                                                            in1=biasb[:, t % 2, a, :], scale=1.0, scalar=MASKED,
                                                            op0=ALU.add, op1=ALU.max, accum_out=st[:, s, 1:2]))
                            V.tensor_scalar(st[:, s, 2:3], st[:, s, 0:1], st[:, s, 1:2], -1.0, ALU.max, ALU.mult)\
                                .then_inc(nm_ready, 1)
                        else:
                            own.link(V.reduce_max(st[:, s, 0:1], ps[:, o + LOC:o + KEYS], AX.X))
                            V.tensor_scalar(st[:, s, 2:3], st[:, s, 0:1], -1.0, None, ALU.mult).then_inc(nm_ready, 1)

                    def sums(i):
                        u = j * per + (ub + i)
                        s, t = i % 2, i // 2
                        dve.wait_ge(p_ready, u + 1)
                        if i >= 2:
                            dve.wait_ge(os_ready, u - 1)
                        if t < QT:
                            own.link(V.tensor_tensor(st[:, s, 5:6], st[:, s, 3:4], st[:, s, 4:5], ALU.add))
                            V.reciprocal(st[:, s, 6:7], st[:, s, 5:6]).then_inc(rinv_ready, 1)
                            dve.wait_ge(pt_ready, u + 1)
                            V.tensor_copy(PT[:, 0:512], ps[:, 4 * BANK:5 * BANK]).then_inc(pt_dve, 1)
                        else:
                            V.reciprocal(st[:, s, 6:7], st[:, s, 4:5]).then_inc(rinv_ready, 1)

                    def place(t):
                        c0 = CTX + t * P if t < QT else (t - QT) * P
                        dve.wait_ge(ot_ready, j * tiles + (ub // 2 + t + 1))
                        y = Y[:, bass.ds(j + 5, 1), c0:c0 + P].rearrange("p a n -> p (a n)")
                        V.tensor_tensor(y, ps[:, 7 * BANK:7 * BANK + P], y, ALU.mult).then_inc(ot_used, 1)

                    maxima(0)
                    for i in range(per):
                        if i + 1 < per:
                            maxima(i + 1)
                        if i and i % 2 == 0:
                            place(i // 2 - 1)
                        sums(i)
                    place(tiles - 1)
                own.leave(PAIRS)
                for c in range(2):
                    ge = g0 + G_CONV + 4 * c
                    dve.wait_ge(evac_done, ge + 2)
                    if c == 0:
                        V.memset(convu[:, 0:1], 0.0)
                        V.memset(convu[:, CTX + 1:CTX + 3], 0.0)
                        V.memset(convu[:, T1 + 3:T1 + 4], 0.0)
                    V.tensor_tensor(convu[:, 1:CTX + 1], ev[:, 0, :CTX], ev[:, 1, :CTX], ALU.mult)
                    own.link(V.tensor_tensor(convu[:, CTX + 3:T1 + 3], ev[:, 0, CTX:], ev[:, 1, CTX:], ALU.mult))
                    taps = [vcol(f"convw{l}", 2 * i + c) for i in range(3)]
                    n = T1 + 2
                    own.link(V.tensor_scalar(convo[:], convu[:, 1:1 + n], taps[1], vcol(f"convb{l}", c), ALU.mult, ALU.add))
                    own.link(V.scalar_tensor_tensor(convo[:], convu[:, 0:n], taps[0], convo[:], ALU.mult, ALU.add))
                    own.link(V.scalar_tensor_tensor(convo[:], convu[:, 2:2 + n], taps[2], convo[:], ALU.mult, ALU.add))
                    dve.wait_ge(evac_done, ge + 4)
                    V.tensor_tensor(ev[:, 2, :CTX], ev[:, 2, :CTX], convo[:, :CTX], ALU.mult)
                    own.link(V.tensor_tensor(ev[:, 2, CTX:], ev[:, 2, CTX:], convo[:, CTX + 2:], ALU.mult))
                    V.tensor_tensor(Y[:, c, :], ev[:, 2, :], ev[:, 3, :], ALU.mult).then_inc(conv_done, 1)
                cs = xcols(l)
                lows(f"y{l}", KD, lambda k: Y[:, k, cs], lambda k: h_hi[:, k, cs], lambda k: h_lo[:, k, cs])
                dve.wait_ge(xr_in, 16 * (l + 1))
                for n in range(KD):
                    dve.wait_ge(evac_done, g0 + G_OUT + n + 1)
                    V.scalar_tensor_tensor(Y[:, n, cs], xin[:, n, cs], ALPHA, stage[:, n % 3, cs], ALU.mult, ALU.add)\
                        .then_inc(xn_ready, 1)
                dve.wait_ge(stat_ready, l + 1)
                for k in range(KD):
                    V.tensor_tensor(Y[:, k, cs], Y[:, k, cs], ps[:, 0:T1 - cs.start], ALU.subtract)\
                        .then_inc(diff_ready, 1)
                dve.wait_ge(std_ready, l + 1)
                own.link(V.reciprocal(stage[:, 2, cs], stage[:, 2, cs]))

                def normed(k):
                    own.link(V.tensor_tensor(Y[:, k, cs], Y[:, k, cs], stage[:, 2, cs], ALU.mult))
                    return V.tensor_scalar(Y[:, k, cs], Y[:, k, cs], vcol(f"lng{l}", k), vcol(f"lnb{l}", k),
                                           ALU.mult, ALU.add)

                def next_input(k):
                    own.link(normed(k))
                    return modulated(1, xin[:, k, :], Y[:, k, :], k)

                if l == 0:
                    lows("h1", KD, lambda k: xin[:, k, :], lambda k: h_hi[:, k, :], lambda k: h_lo[:, k, :], next_input)
                else:
                    for k in range(KD):
                        normed(k).then_inc(xn_ready, 1)

            def rsqrt(count, buf):
                dve.wait_ge(std_ready, count)
                own.link(V.reciprocal(buf, buf))

            rs = T2[:, 2, :]
            rsqrt(3, rs)
            lows("h2", KD, lambda k: C2[:, 8 + k, :], lambda k: g_hi[:, k, :], lambda k: g_lo[:, k, :],
                 lambda k: V.scalar_tensor_tensor(C2[:, 8 + k, :], Y[:, k, CTX:], vcol("g_mix_pre", k), rs,
                                                  ALU.mult, ALU.mult))
            dve.wait_ge(xs_out, 32)
            own.link(V.memset(xb[:, 0:3], 0.0))
            xc = B2[:, 0, :]
            for c in range(8):
                dve.wait_ge(evac_done, G_RNN + 2 * c + 1)
                tap = lambda i: vcol("rconvw", 8 * i + c)
                own.link(V.tensor_scalar(xc, xb[:, 0:SEQ], tap(0), vcol("rconvb", c), ALU.mult, ALU.add))
                for i in (1, 2):
                    own.link(V.scalar_tensor_tensor(xc, xb[:, i:i + SEQ], tap(i), xc, ALU.mult, ALU.add))
                V.scalar_tensor_tensor(xc, xb[:, 3:], tap(3), xc, ALU.mult, ALU.add).then_inc(rnn_xc, 1)
                dve.wait_ge(rnn_m2, c + 1)
                dve.wait_ge(rnn_xc, c + 1)
                dve.wait_ge(sp_lo, SPLITS["rnn"] + c)
                own.link(V.tensor_scalar(B2[:, 6, :], B2[:, 5, :], 1.0, None, ALU.add))
                own.link(V.reciprocal(B2[:, 6, :], B2[:, 6, :]))
                V.scalar_tensor_tensor(B2[:, 6, :], B2[:, 5, :], 2.0, B2[:, 6, :], ALU.mult, ALU.mult).then_inc(rnn_mult, 1)
                own.link(V.tensor_tensor(B2[:, 3, :], B2[:, 3, :], xc, ALU.mult))
                dve.wait_ge(rnn_mult, 2 * c + 2)
                own.link(V.memset(B2[:, 7, 0:1], 1.0))
                own.link(V.tensor_tensor(B2[:, 3, :], B2[:, 3, :], B2[:, 7, :], ALU.mult))
                own.link(V.tensor_tensor_scan(B2[:, 5, :], B2[:, 4, :], B2[:, 3, :], 0.0, ALU.mult, ALU.add))
                dve.wait_ge(evac_done, G_RNN + 2 * c + 2)
                V.tensor_tensor(B2[:, 6, :], B2[:, 5, :], B2[:, 1, :], ALU.mult).then_inc(sp_tmp, 1)
                dve.wait_ge(sp_hi, SPLITS["rnn"] + c + 1)
                V.tensor_tensor(r_lo[:, c, :], B2[:, 6, :], r_hi[:, c, :].bitcast(F32), ALU.subtract).then_inc(sp_lo, 1)
            for n in range(KD):
                dve.wait_ge(evac_done, G_RMIX + 2 * n + 2)
                V.tensor_tensor(B2[:, n, :], T2[:, n % 2, :], T2[:, 2 + n % 2, :], ALU.mult).then_inc(mix_used, 1)
            dve.wait_ge(slab_done, G_POOL)
            for buf in (pu, pa, pb):
                own.link(V.memset(buf[:, 0:16], 0.0))
            dve.wait_ge(tab_in, 144)
            for c in range(4):
                dve.wait_ge(evac_done, G_POOL + c + 1)
                if c:
                    dve.wait_ge(pool_d, c)
                s = pu
                for i in range(c + 1):
                    dst, sh = (pa, pb)[i % 2], 1 << i
                    own.link(V.tensor_tensor(dst[:, 16:], s[:, 16:], s[:, 16 - sh:16 + SEQ - sh], ALU.add))
                    s = dst
                if c:
                    dve.wait_ge(pool_ps, c)
                own.link(V.tensor_tensor(C2[:, 12, :16], s[:, 16:32], C2[:, 14, 16 * c:16 * c + 16], ALU.mult))
                V.tensor_tensor(C2[:, 12, :16], C2[:, 12, :16], pu[:, 16:32], ALU.subtract)
                V.scalar_tensor_tensor(C2[:, 12, 16:], s[:, 32:], 1.0 / (2 << c), pu[:, 32:], ALU.mult, ALU.subtract)\
                    .then_inc(pool_d, 1)
                if c:
                    dve.wait_ge(sp_hi, SPLITS["pool"] + c)
                    V.tensor_tensor(r_lo[:, c - 1, :], C2[:, 13, :], r_hi[:, c - 1, :].bitcast(F32), ALU.subtract)\
                        .then_inc(sp_lo, 1)
            dve.wait_ge(sp_hi, SPLITS["pool"] + 4)
            V.tensor_tensor(r_lo[:, 3, :], C2[:, 13, :], r_hi[:, 3, :].bitcast(F32), ALU.subtract).then_inc(sp_lo, 1)
            for n in range(KD):
                dve.wait_ge(evac_done, G_PMIX + 2 * n + 2)
                own.link(V.tensor_tensor(T2[:, n % 2, :], T2[:, n % 2, :], T2[:, 2 + n % 2, :], ALU.mult))
                V.tensor_tensor(B2[:, n, :], B2[:, n, :], T2[:, n % 2, :], ALU.add).then_inc(mix_used, 1)
            lows("merged", KD, lambda k: B2[:, k, :], lambda k: g_hi[:, k, :], lambda k: g_lo[:, k, :])
            dve.wait_ge(xr_in, 48)
            rsqrt(4, rs)
            for k in range(KD):
                own.link(V.scalar_tensor_tensor(C2[:, k, :], C2[:, k, :], vcol("g_mix_post", k), rs, ALU.mult, ALU.mult))
                V.tensor_tensor(B2[:, k, :], B2[:, k, :], C2[:, k, :], ALU.add).then_inc(xn_ready, 1)
            rsqrt(5, rs)
            lows("h3", KD, lambda k: C2[:, k, :], lambda k: g_hi[:, k, :], lambda k: g_lo[:, k, :],
                 lambda k: V.scalar_tensor_tensor(C2[:, k, :], B2[:, k, :], vcol("g_ffn_pre", k), rs, ALU.mult, ALU.mult))
            own.link(V.memset(gpad[:, 0:2], 0.0))
            for f in range(FF_GROUPS):
                gf = G_FFN + 24 * f
                for c in range(FF_CHUNKS):
                    cc = FF_CHUNKS * f + c
                    dve.wait_ge(evac_done, gf + 2 * c + 1)
                    own.link(V.tensor_scalar(ffc[:], gpad[:, 2:], vcol("fconvw", 48 + cc), None, ALU.mult))
                    own.link(V.scalar_tensor_tensor(ffc[:], gpad[:, 1:1 + SEQ], vcol("fconvw", 24 + cc), ffc[:],
                                                    ALU.mult, ALU.add))
                    V.scalar_tensor_tensor(ffc[:], gpad[:, 0:SEQ], vcol("fconvw", cc), ffc[:], ALU.mult, ALU.add)\
                        .then_inc(ff_conv, 1)
                    dve.wait_ge(ff_gelu, cc + 1)
                    dve.wait_ge(evac_done, gf + 2 * c + 2)
                    dve.wait_ge(sp_lo, SPLITS[f"hid{f}"] + c)
                    V.tensor_tensor(fft[:], ffc[:], ffu[:], ALU.mult).then_inc(sp_tmp, 1)
                    dve.wait_ge(sp_hi, SPLITS[f"hid{f}"] + c + 1)
                    V.tensor_tensor(r_lo[:, c, :], fft[:], r_hi[:, c, :].bitcast(F32), ALU.subtract).then_inc(sp_lo, 1)
                if f:
                    for n in range(KD):
                        dve.wait_ge(evac_done, gf + 16 + n + 1)
                        V.tensor_tensor(B2[:, n, :], B2[:, n, :], (ffu, fft)[n % 2][:], ALU.add).then_inc(acc_used, 1)
            rsqrt(6, rs)
            dve.wait_ge(xr_in, 64)
            for k in range(KD):
                own.link(V.scalar_tensor_tensor(B2[:, k, :], B2[:, k, :], vcol("g_ffn_post", k), rs, ALU.mult, ALU.mult))
                V.tensor_tensor(B2[:, k, :], B2[:, k, :], C2[:, k, :], ALU.add).then_inc(xn_ready, 1)
            rs2 = C2[:, 7, :]
            rsqrt(7, rs2)
            lows("p", 2, lambda k: C2[:, k, :], lambda k: p_hi[:, k, :], lambda k: p_lo[:, k, :])
            lows("h4", KD, lambda k: C2[:, 8 + k, :], lambda k: g_hi[:, k, :], lambda k: g_lo[:, k, :],
                 lambda k: V.scalar_tensor_tensor(C2[:, 8 + k, :], B2[:, k, :], vcol("g_ple_gate", k), rs2,
                                                  ALU.mult, ALU.mult))
            rsqrt(8, rs)
            for n in range(KD):
                own.link(V.scalar_tensor_tensor(C2[:, n, :], C2[:, n, :], vcol("g_ple_post", n), rs, ALU.mult, ALU.mult))
                dve.wait_ge(evac_done, G_PLEG + n + 1)
                own.link(V.tensor_tensor(C2[:, n, :], C2[:, n, :], T2[:, n % 2, :], ALU.mult))
                V.tensor_tensor(B2[:, n, :], B2[:, n, :], C2[:, n, :], ALU.add).then_inc(out_ready, 1)


def slabs(w):
    k, n = w.shape
    return w.reshape(k // P, P, n // P, P).transpose(2, 1, 0, 3).reshape(n // P, P, k)


def features(v):
    v = v.reshape(-1, P)
    return v.T


def constants():
    f = np.float32
    ident = np.eye(P, dtype=f)
    ones = np.full((P, P), 1.0 / D, f)
    blk = np.kron(np.eye(2, dtype=f), np.full((HD, HD), 1.0 / HD, f))
    mats = np.stack([ident, ones, blk], 1)
    rot = np.zeros((P, P), f)
    d = np.arange(P)
    for m in range(P):
        if m % 32 < 16:
            rot[m + 16, m] = -1.0
        else:
            rot[m - 16, m] = 1.0
    i = np.arange(P)
    ahead = np.maximum(i[None, :] - i[:, None], 0)
    behind = np.maximum(i[:, None] - i[None, :], 0)
    rets = np.stack([rot, ahead, behind, np.tile(i + 1, (P, 1)), np.tile(P - i, (P, 1))], 1).astype(f)
    nf = HD // 4
    inv = f(10000.0) ** (-np.arange(nf, dtype=f) / f(nf))
    t = np.arange(SEQ)
    row, col = (t // GRID_W).astype(f), (t % GRID_W).astype(f)
    ang = np.where((d % HD < 32)[:, None], row[None, :], col[None, :]) * inv[d % nf][:, None]
    ropes = np.stack([np.cos(ang), np.sin(ang)]).astype(f)
    tab = np.zeros((4, 16), f)
    for g in range(4):
        tab[g] = 1.0 / np.minimum(np.arange(16) + 1, 2 << g)
    pooltab = np.tile(tab.reshape(1, 64), (P, 1))
    cols = np.stack([P - 1 - i, i], 1).astype(f)
    eps = np.tile(np.array([[LN_EPS, RMS_EPS]], f), (P, 1))
    return mats, rets, ropes, pooltab, cols, eps


def bias_layout(rpb):
    L, H = rpb.shape[:2]
    q = np.arange(P)
    kk = np.arange(LOC)
    out = np.empty((L, PAIRS, QT, P, 2, LOC), np.float32)
    for t in range(QT):
        k0 = min(max(t - 2, 0), QT - KEYT)
        r, c = 2 * t + q // GRID_W, q % GRID_W
        kr, kc = 2 * k0 + kk // GRID_W, kk % GRID_W
        rs = np.clip(r - WIN_H // 2, 0, ROWS - WIN_H)
        cs = np.clip(c - WIN_W // 2, 0, GRID_W - WIN_W)
        ok = ((kr[None] >= rs[:, None]) & (kr[None] < rs[:, None] + WIN_H)
              & (kc[None] >= cs[:, None]) & (kc[None] < cs[:, None] + WIN_W))
        dr = np.where(ok, kr[None] - r[:, None] + WIN_H - 1, 0)
        dc = np.where(ok, kc[None] - c[:, None] + WIN_W - 1, 0)
        part = np.where(ok[None, None], rpb[:, :, dr, dc], np.float32(MASKED))
        out[:, :, t] = part.reshape(L, PAIRS, 2, P, LOC).transpose(0, 1, 3, 2, 4)
    return out.reshape(L * PAIRS * QT, P, 2, LOC)


def kernel(**inputs):
    import concourse.bacc as _bacc
    from concourse.bass_utils import run_bass_kernel_spmd as _run

    a = {k: np.asarray(v) for k, v in inputs.items()}
    mats, rets, ropes, pooltab, cols, eps = constants()
    xall = np.concatenate([a["ctx"][0], a["x"][0]], 0)
    xT = xall.T.reshape(KD, P, T1)
    cT = np.stack([a["c"][0], a["c_ctx"]], 1).reshape(KD, P, 2).transpose(1, 0, 2).reshape(P, 2 * KD)
    modw = np.concatenate([slabs(a["w_mod"][l]) for l in range(2)])
    vals = {"cols": cols, "eps": eps}
    bm = a["b_mod"].reshape(48, P).T
    vals["bmod"] = np.stack([bm, bm], 2).reshape(P, 96)
    for l in range(2):
        vals[f"convw{l}"] = features(a["conv_w"][l])
        vals[f"convb{l}"] = features(a["conv_b"][l])
        vals[f"lng{l}"] = features(a["ln_g"][l])
        vals[f"lnb{l}"] = features(a["ln_b"][l])
        dl = a["ret_decay"][l]
        wide = np.broadcast_to(dl.reshape(1, 12), (P, 12))
        two = np.repeat(dl.reshape(2, PAIRS, 2), HD, axis=2).reshape(2 * PAIRS, P).T
        vals[f"dec{l}"] = np.concatenate([wide, two], 1)
    vals["lam"] = features(a["lru_lambda_2"][0])
    for n in ("g_mix_pre", "g_mix_post", "g_ffn_pre", "g_ffn_post", "g_ple_gate", "g_ple_post", "pool_scale"):
        vals[n] = features(a[n + "_2"][0])
    vals["rconvw"] = features(a["conv_w_2"][0])
    vals["rconvb"] = features(a["conv_b_2"][0])
    vals["b_gates"] = features(a["b_rg_gates_2"][0])
    vals["fconvw"] = features(a["ffn_conv_w_2"][0])
    vals["fconvb"] = features(a["ffn_conv_b_2"][0])
    vecs = np.concatenate([vals[n] for n in VEC], 1)
    assert vecs.shape == (P, NVEC)

    parts = []
    for l in range(2):
        s = slabs(a["w_in"][l])
        rk, rv, nk, nv, rq, rg, nq, ng = (s[3 * i:3 * i + 3] for i in range(8))
        ch, cb, ccg, cz = (s[24 + 2 * i:26 + 2 * i] for i in range(4))
        parts += [rk, rq, rv, rg, nk, nq, nv, ng]
        for c in range(2):
            parts += [ccg[c:c + 1], ch[c:c + 1], cb[c:c + 1], cz[c:c + 1]]
        parts.append(slabs(a["w_out"][l]))
    s = slabs(a["w_in_2"][0])
    pool_u, rx, rg, gp, gr = s[0:4], s[4:12], s[12:20], s[20:28], s[28:36]

    def braid(u, v):
        return np.stack([u, v], 1).reshape((-1,) + u.shape[1:])

    up = slabs(a["w_up_2"][0])
    down = a["w_down_2"][0]
    parts += [braid(rx, rg), braid(gr, slabs(a["w_rg_out_2"][0])), pool_u, gp, slabs(a["w_o_2"][0])]
    for f in range(FF_GROUPS):
        parts += [braid(up[8 * f:8 * f + 8], up[24 + 8 * f:32 + 8 * f]), slabs(down[D * f:D * (f + 1)])]
    parts.append(slabs(a["w_ple_gate_2"][0]))
    s8 = np.concatenate(parts)
    assert s8.shape[0] == S8_END
    s4 = slabs(a["w_pool_out_2"][0])
    s2 = slabs(a["w_ple_proj_2"][0])
    wg = a["w_rg_gates_2"][0].reshape(2, 8, 2, HD, HD)
    rgw = np.zeros((2, 8, P, P), np.float32)
    rgw[:, :, :HD, :HD] = wg[:, :, 0]
    rgw[:, :, HD:, HD:] = wg[:, :, 1]
    pT = a["p_2"][0, 0].T.reshape(2, P, SEQ)
    arrays = {"xT": xT, "cT": cT, "modw": modw, "vecs": vecs, "mats": mats, "ropes": ropes, "rets": rets,
              "bias": bias_layout(a["na_rpb"]), "s8": s8, "s4": s4, "s2": s2, "rgw": rgw.reshape(16, P, P),
              "poolw": a["pool_w_2"][0], "pooltab": pooltab, "pT": pT}
    nc = _bacc.Bacc("TRN2", target_bir_lowering=False, num_devices=1)
    ins, args = {}, []
    for name, v in arrays.items():
        v = np.ascontiguousarray(v)
        ins[name] = v
        args.append(nc.dram_tensor(name, v.shape, F32, kind="ExternalInput").ap())
    args.append(nc.dram_tensor("outT", (KD, P, SEQ), F32, kind="ExternalOutput").ap())
    build_kernel(nc, *args)
    r = _run(nc, [ins], core_ids=[0])
    out = np.asarray(r.results[0]["outT"])
    return np.ascontiguousarray(out.reshape(D, SEQ).T)[None]
```

```python
from contextlib import ExitStack

import numpy as np
import concourse.bass as bass
from concourse import mybir

F32 = mybir.dt.float32
F32R = mybir.dt.float32r
ALU = mybir.AluOpType
ACT = mybir.ActivationFunctionType
AX = mybir.AxisListType

P = 128
D = 1024
KD = D // P
SEQ = 1024
CTX = 256
T1 = CTX + SEQ
NT = T1 // P
NC = CTX // P
HD = 64
PAIRS = 3
GRID_W, WIN_H, WIN_W = 64, 8, 16
ROWS = SEQ // GRID_W
QT = SEQ // P
KEYT = 5
LOC = KEYT * P
KEYS = LOC + CTX
ALPHA = 4.0 ** 0.25
LN_EPS, RMS_EPS = 1e-5, 1e-6
LRU_C = 8.0
MASKED = -1e30
FF_GROUPS, FF_CHUNKS = 3, 8

L_SLABS = 40
G_RET, G_NA, G_CONV, G_OUT = 0, 12, 24, 32
G_RNN = 2 * L_SLABS
G_RMIX = G_RNN + 16
G_POOL = G_RMIX + 16
G_PMIX = G_POOL + 4
G_WO = G_PMIX + 16
G_FFN = G_WO + 8
G_PLEP = G_FFN + FF_GROUPS * 24
G_PLEG = G_PLEP + 8
G_END = G_PLEG + 8
S8_GP = G_PMIX
S8_WO = S8_GP + 8
S8_PLEG = S8_WO + 8 + FF_GROUPS * 24
S8_END = S8_PLEG + 8

MOD_FIRST, MOD_ALL = 16, 48

SPLITS = {}
_at = 0
for _name, _n in (("h0", 8), ("y0", 8), ("h1", 8), ("y1", 8), ("h2", 8), ("rnn", 8), ("pool", 4),
                  ("merged", 8), ("h3", 8), ("hid0", 8), ("hid1", 8), ("hid2", 8), ("p", 2), ("h4", 8)):
    SPLITS[_name] = _at
    _at += _n

VEC = {}
_at = 0
for _name, _n in (("bmod", 96), ("dec0", 18), ("dec1", 18), ("lam", 8), ("cols", 2),
                  ("convw0", 6), ("convb0", 2), ("lng0", 8), ("lnb0", 8),
                  ("convw1", 6), ("convb1", 2), ("lng1", 8), ("lnb1", 8),
                  ("g_mix_pre", 8), ("g_mix_post", 8), ("g_ffn_pre", 8), ("g_ffn_post", 8), ("g_ple_gate", 8),
                  ("g_ple_post", 8), ("pool_scale", 4), ("rconvw", 32), ("rconvb", 8), ("b_gates", 16),
                  ("fconvw", 72), ("fconvb", 24), ("eps", 2)):
    VEC[_name] = (_at, _n)
    _at += _n
NVEC = _at

TEMPS = {}
_at = 0
for _name in ("h0", "h1", "h2", "rnn", "h3", "hid0", "hid1", "hid2", "h4"):
    TEMPS[_name] = _at
    _at += 8


OUT_TILES = [[(0, 2), (2, 4), (6, 4)], [(2, 2), (4, 3), (7, 3)]]
BACK = [1, 0] + list(range(NT - 1, NC, -1))
STATE_AT = [lambda n: n - 1, lambda n: 0 if n == 0 else NT - n]


def o_groups(layer, pair):
    return 3 * (3 * layer + pair)


class Chain:

    def __init__(self, eng, sem):
        self.eng, self.sem, self.n, self.j, self.per, self.m = eng, sem, 0, None, 0, 0

    def count(self):
        return self.n if self.j is None else self.j * self.per + (self.n + self.m)

    def step(self, ins):
        ins.then_inc(self.sem, 1)
        if self.j is None:
            self.n += 1
        else:
            self.m += 1

    def link(self, ins):
        self.step(ins)
        self.eng.wait_ge(self.sem, self.count())

    def enter(self, j, per):
        self.j, self.per, self.m = j, per, 0

    def leave(self, turns):
        assert self.m == self.per, (self.m, self.per)
        self.n += turns * self.per
        self.j = None


def build_kernel(nc, xT, cT, modw, vecs, mats, ropes, rets, bias, s8, s4, s2, rgw, poolw, pooltab, pT, outT):
    V, A, T, G = nc.vector, nc.scalar, nc.tensor, nc.gpsimd
    with ExitStack() as ctx:
        arena = ctx.enter_context(nc.sbuf_tensor("arena", [P, 53208], F32))
        base = 229344 - 53208 * 4

        def at(name, word, shape, dt=F32):
            size = int(np.prod(shape[1:]))
            assert word + size <= 53208, name
            return nc.alloc_sbuf_tensor_at(name, shape, dt, offset=base + 4 * word)

        W_A, W_B, W_C = 0, 2 * KD * T1, 3 * KD * T1
        C_SIZE = 15232
        W_RING = W_C + C_SIZE
        W_SMALL = W_RING + 6 * 1024
        h_hi = at("h_hi", W_A, [P, KD, T1], F32R)
        h_lo = at("h_lo", W_A + KD * T1, [P, KD, T1], F32R)
        Y = at("Y", W_B, [P, KD, T1])
        QK = at("QK", W_C, [P, 6, T1])
        Vt = at("Vt", W_C + 6 * T1, [P, NT, 3 * P])
        W_CT = W_C + 6 * T1 + NT * 3 * P
        modfirst = at("modfirst", W_A, [P, MOD_FIRST, KD * P])
        modring = at("modring", W_B, [P, 2, KD * P])
        modring6 = at("modring6", W_C + 7712, [P, 6, KD * P])
        cosT = at("cosT", W_CT, [P, SEQ])
        sinT = at("sinT", W_CT + SEQ, [P, SEQ])
        rope_tmp = at("rope_tmp", W_CT + 2 * SEQ, [P, SEQ])
        ret_const = at("ret_const", W_CT + 3 * SEQ, [P, 5, P])
        Dm = at("Dm", W_CT, [P, 6, P])
        WQ = at("WQ", W_CT + 768, [P, 2, 3, P])
        dtmp = at("dtmp", W_CT + 2304, [P, 6, P])
        qw = [at("qw0", W_CT + 2304, [P, 2, 4 * P]), at("qw1", W_B + 1024, [P, 2, 4 * P])]
        kw = at("kw", W_B, [P, 2, NT, P])
        W_YNA = W_B + 5 * T1
        VT = at("VT", W_YNA, [P, 3, T1])
        ST = at("ST", W_YNA, [P, 2, NT, P])
        SD = [at("SD0", W_YNA + 2 * T1, [P, 2, 4 * P]), at("SD1", W_B, [P, 2, 4 * P])]
        hn_tmp = at("hn_tmp", W_B, [P, 2, T1])
        biasb = at("biasb", W_CT, [P, 2, 2, LOC])
        Sb = [at("Sb0", W_CT + 4 * LOC, [P, KEYS]), at("Sb1", W_B + KEYS, [P, KEYS])]
        PT = at("PT", W_B, [P, KEYS])
        QZ = at("QZ", W_B + 2 * KEYS, [P, 2, 2, P])
        OS = at("OS", W_B + 2 * KEYS + 512, [P, 2, P])
        ev = at("ev", W_C, [P, 4, T1])
        convu = at("convu", W_C + 4 * T1, [P, T1 + 4])
        convo = at("convo", W_C + 5 * T1 + 8, [P, T1 + 2])
        xin = at("xin", W_C, [P, KD, T1])
        stage = at("stage", W_C + 8 * T1, [P, 3, T1])
        y_sum = stage[:, 2, :]
        g_hi = at("g_hi", 0, [P, KD, SEQ], F32R)
        g_lo = at("g_lo", 8192, [P, KD, SEQ], F32R)
        B2 = at("B2", 16384, [P, KD, SEQ])
        r_hi = at("r_hi", 24576, [P, KD, SEQ], F32R)
        r_lo = at("r_lo", 32768, [P, KD, SEQ], F32R)
        sq_g = at("sq_g", 0, [P, KD, SEQ])
        C2 = at("C2", 24576, [P, 2 * KD, SEQ])
        W_T2 = 40960
        T2 = at("T2", W_T2, [P, 4, SEQ])
        xb = at("xb", W_T2, [P, SEQ + 3])
        rgwt = at("rgwt", W_T2 + 1032, [P, 16, P])
        xcs = [B2[:, 0, :], at("xc1", W_T2 + 3088, [P, SEQ])[:]]
        gpad = at("gpad", W_T2, [P, SEQ + 2])
        ffu = at("ffu", W_T2 + 1032, [P, SEQ])
        ffc = at("ffc", W_T2 + 2056, [P, SEQ])
        fft = at("fft", W_T2 + 3080, [P, SEQ])
        pu = at("pu", 28672, [P, SEQ + 16])
        pa = at("pa", 28672 + 1040, [P, SEQ + 16])
        pb = at("pb", 28672 + 2080, [P, SEQ + 16])
        p_hi = at("p_hi", W_T2, [P, 2, SEQ], F32R)
        p_lo = at("p_lo", W_T2 + 2048, [P, 2, SEQ], F32R)
        raw = [at(f"raw{s}", W_RING + 1024 * s, [P, KD * P]) for s in range(2)]
        w_hi = [at(f"w_hi{s}", W_RING + 2048 + 1024 * s, [P, KD * P], F32R) for s in range(2)]
        w_lo = [at(f"w_lo{s}", W_RING + 4096 + 1024 * s, [P, KD * P], F32R) for s in range(2)]
        cm = at("cm", W_SMALL, [P, 3, P])
        vec = at("vec", W_SMALL + 384, [P, NVEC])
        w = W_SMALL + 384 + (NVEC + 7) // 8 * 8
        cact = at("cact", w, [P, 3, KD * 2])
        mod = at("mod", w + 48, [P, 48, 2])
        lg = at("lg", w + 144, [P, 44])
        lru_c = at("lru_c", w + 192, [P, 2, 8])
        wk = at("wk", w + 208, [P, 12])
        gch = at("gch", w + 224, [P, 6])
        st = at("st", w + 232, [P, 2, 8])
        pool_zero = at("pool_zero", w + 248, [P, 8])
        mod_ln = at("mod_ln", w + 256, [P, 16, 2])
        lgt = at("lgt", W_CT, [P, 6, 44])
        ident, ones, blk = cm[:, 0, :], cm[:, 1, :], cm[:, 2, :]

        def vcol(name, i, n=1):
            o, size = VEC[name]
            assert i + n <= size
            return vec[:, o + i:o + i + n]

        ps = ctx.enter_context(nc.psum_tensor("ps", [P, 8 * 512], F32))
        BANK = 512

        x_saved = nc.dram_tensor("x_saved", [KD, P, T1], F32).ap()

        sems = {}

        def sem(name):
            sems[name] = ctx.enter_context(nc.semaphore(name))
            return sems[name]

        raw_loaded = [sem("raw_loaded0"), sem("raw_loaded1")]
        zero_set = sem("zero_set")
        hi_done, split_done = sem("hi_done"), sem("split_done")
        slab_done, evac_done = sem("slab_done"), sem("evac_done")
        const_in, x_in, mod_in = sem("const_in"), [sem(f"x_in{i}") for i in range(4)], [sem(f"mod_in{i}") for i in range(8)]
        modring_in = [sem("modring_in0"), sem("modring_in1")]
        cact_ready, mod_used = sem("cact_ready"), sem("mod_used")
        sp_tmp, sp_hi, sp_lo = sem("sp_tmp"), sem("sp_hi"), sem("sp_lo")
        dve_step, act_step = sem("dve_step"), sem("act_step")
        tab_in, rot_ready, rope_done = sem("tab_in"), sem("rot_ready"), sem("rope_done")
        vt_ready, vt_used = sem("vt_ready"), sem("vt_used")
        kt_ready, kt_used = sem("kt_ready"), sem("kt_used")
        lg_ready, dtab, wtab = sem("lg_ready"), sem("dtab"), sem("wtab")
        u_ready, state_ready = sem("u_ready"), sem("state_ready")
        qw_ready = sem("qw_ready")
        sc_ready, sd_ready, o_ready, o_used = sem("sc_ready"), sem("sd_ready"), sem("o_ready"), sem("o_used")
        hn_mean, hn_diff, hn_sq, hn_var, hn_std, hn_done = (sem("hn_mean"), sem("hn_diff"), sem("hn_sq"),
                                                            sem("hn_var"), sem("hn_std"), sem("hn_done"))
        bias_in = [sem("bias_in0"), sem("bias_in1")]
        qz_ready, s_ready, nm_ready = sem("qz_ready"), sem("s_ready"), sem("nm_ready")
        p_ready, pt_ready, pt_dve, pt_act = sem("p_ready"), sem("pt_ready"), sem("pt_dve"), sem("pt_act")
        rinv_ready, pv_ready, os_ready, ot_ready, ot_used = (sem("rinv_ready"), sem("pv_ready"), sem("os_ready"),
                                                             sem("ot_ready"), sem("ot_used"))
        qz_clear = sem("qz_clear")
        conv_done = sem("conv_done")
        xr_in, xs_out = sem("xr_in"), sem("xs_out")
        stat_sq, stat_used, stat_ready, std_ready = (sem("stat_sq"), sem("stat_used"), sem("stat_ready"),
                                                               sem("std_ready"))
        diff_ready, xn_ready = sem("diff_ready"), sem("xn_ready")
        sq_added, y_added = sem("sq_added"), sem("y_added")
        rnn_xc, rnn_gates, rnn_act, rnn_m2, rnn_mult = (sem("rnn_xc"), sem("rnn_gates"), sem("rnn_act"),
                                                                  sem("rnn_m2"), sem("rnn_mult"))
        mix_used, pool_d, pool_ps = sem("mix_used"), sem("pool_d"), sem("pool_ps")
        ff_conv, ff_gelu, acc_used, out_ready, out_done = (sem("ff_conv"), sem("ff_gelu"),
                                                                    sem("acc_used"), sem("out_ready"), sem("out_done"))
        block = ctx.enter_context(nc.Block())

        CUTS = (0, 14, L_SLABS + 14, G_PMIX)
        RUNS = [(g, (CUTS[i + 1] - g) // 2, (s8, g, 2), (s8, g + 1, 2), KD, KD) for i, g in enumerate(CUTS[:3])] + [
                (G_PMIX, 8, (s8, S8_GP, 1), (s4, 0, 1), KD, 4),
                (G_WO, 40, (s8, S8_WO, 2), (s8, S8_WO + 1, 2), KD, KD),
                (G_PLEP, 4, (s2, 0, 2), (s2, 1, 2), 2, 2),
                (G_PLEG, 4, (s8, S8_PLEG, 2), (s8, S8_PLEG + 1, 2), KD, KD)]

        @block.sync
        def _(sp):
            def load(g, s, array, place, k):
                sp.dma_start(raw[s][:, :k * P], array[bass.ds(place, 1)].rearrange("a p n -> p (a n)"))\
                    .then_inc(raw_loaded[s], 16)

            for i in range(0, 8, 2):
                sp.dma_start(modfirst[:, 2 * i:2 * i + 2, :], modw[2 * i:2 * i + 2].rearrange("a p n -> p a n"))\
                    .then_inc(mod_in[i], 16)
            load(0, 0, s8, 0, KD)
            load(1, 1, s8, 1, KD)
            for i in range(0, 4, 2):
                sp.dma_start(Y[:, 2 * i:2 * i + 2, :], xT[2 * i:2 * i + 2].rearrange("k p t -> p k t"))\
                    .then_inc(x_in[i], 16)
            for g0, pairs, a0, a1, k0, k1 in RUNS:
                lo = 1 if g0 == 0 else 0
                with sp.Fori(lo, pairs) as j:
                    for s, (array, place, step), k in ((0, a0, k0), (1, a1, k1)):
                        sp.wait_ge(split_done, j * 2 + (g0 + s - 1))
                        load(None, s, array, j * step + place, k)
            for n in range(KD):
                sp.wait_ge(out_ready, n + 1)
                sp.dma_start(outT[n], B2[:, n, :]).then_inc(out_done, 16)
            sp.wait_ge(out_done, 16 * KD)

        @block.gpsimd
        def _(pool):
            zero = pool_zero[:, 0:1]
            G.memset(zero, 0.0).then_inc(zero_set, 1)
            pool.wait_ge(zero_set, 1)

            def split(s, k, g):
                n = k * P
                G.tensor_tensor(w_hi[s][:, :n], raw[s][:, :n], zero.to_broadcast([P, n]), ALU.add).then_inc(hi_done, 1)
                pool.wait_ge(hi_done, g + 1)
                G.tensor_tensor(w_lo[s][:, :n], raw[s][:, :n], w_hi[s][:, :n].bitcast(F32), ALU.subtract)\
                    .then_inc(split_done, 1)

            def weighted_queries(l):
                pool.wait_ge(wtab, l + 1)
                for p in range(PAIRS):
                    q = o_groups(l, p)
                    for i, (n0, cnt) in enumerate(OUT_TILES[l]):
                        if i == 1:
                            pool.wait_ge(u_ready, 2 * (3 * l + p) + 2)
                        elif q + i:
                            pool.wait_ge(o_ready, q + (1 if i else 0))
                        qs = QK[:, 3 + p, n0 * P:(n0 + cnt) * P].rearrange("p (t f) -> p t f", f=P)
                        for d in range(2):
                            last = G.tensor_tensor(qw[i % 2][:, d, :cnt * P].rearrange("p (t f) -> p t f", f=P), qs,
                                                   WQ[:, d, p, :].unsqueeze(1).to_broadcast([P, cnt, P]), ALU.mult)
                        last.then_inc(qw_ready, 1)

            for g0, pairs, a0, a1, k0, k1 in RUNS:
                if g0 == 0:
                    for s in range(2):
                        pool.wait_ge(raw_loaded[s], 16)
                        split(s, KD, s)
                lo = 1 if g0 == 0 else 0
                with pool.Fori(lo, pairs) as j:
                    for s, k in ((0, k0), (1, k1)):
                        g = j * 2 + (g0 + s)
                        pool.wait_ge(raw_loaded[s], j * 16 + (8 * g0 + 16))
                        pool.wait_ge(slab_done, g - 1)
                        split(s, k, g)
                if g0 + 2 * pairs in CUTS[1:3]:
                    weighted_queries(CUTS.index(g0 + 2 * pairs) - 1)

        FULL = [(0, 0, 512), (512, 512, 512), (1024, 1024, 256)]
        XONLY = [(CTX, 0, 512), (CTX + 512, 512, 512)]
        XPART = [(CTX, CTX, 512 - CTX), (512, 512, 512), (1024, 1024, 256)]
        SEC = [(0, 0, 512), (512, 512, 512)]
        GROUPS = [(0, 4), (4, 4), (8, 2)]
        HN_SEGS = [[(0, 512), (512, 512), (1024, 256)], [(CTX, 512), (CTX + 512, 512)]]
        HN_AT = [[1, 6, 11], [1, 8]]

        @block.tensor
        def _(pe):
            def slab(g, s, hi, lo, k_n, segs, slot, ready=None, first=False, between=None):
                pe.wait_ge(split_done, g + 1)
                if not first:
                    pe.wait_ge(evac_done, g - 1)
                o = s * slot * BANK
                for k in range(k_n):
                    if ready is not None:
                        pe.wait_ge(sp_lo, ready + k + 1)
                    kk = slice(k * P, (k + 1) * P)
                    for wt, xx, n in ((w_hi, hi, 0), (w_hi, lo, 1), (w_lo, hi, 2)):
                        for t0, c0, size in segs:
                            last = T.matmul(ps[:, o + c0:o + c0 + size], wt[s][:, kk], xx[:, k, t0:t0 + size],
                                            start=(k == 0 and n == 0), stop=(k == k_n - 1 and n == 2))
                    if k == k_n - 1:
                        last.then_inc(slab_done, 1)
                    if between is not None:
                        between(k)

            def gemm(g0, n, hi, lo, segs, slot, ready):
                for s in range(2):
                    slab(g0 + s, s, hi, lo, KD, segs, slot, ready if s == 0 else None, first=(g0 == 0))
                if n > 2:
                    with pe.Fori(1, n // 2) as j:
                        for s in range(2):
                            slab(j * 2 + (g0 + s), s, hi, lo, KD, segs, slot)

            pe.wait_ge(const_in, 48)
            pe.wait_ge(cact_ready, 1)

            def modulation(column, weights):
                for k in range(KD):
                    last = T.matmul(ps[:, column], weights[:, k * P:(k + 1) * P], cact[:, 2, 2 * k:2 * k + 2],
                                    start=(k == 0), stop=(k == KD - 1))
                last.then_inc(mod_used, 1)

            for m in range(MOD_FIRST):
                if m % 2 == 0:
                    pe.wait_ge(mod_in[m // 2], 16)
                modulation(slice(7 * BANK + 2 * m, 7 * BANK + 2 * m + 2), modfirst[:, m, :])

            def beyond(s):
                return (3 * (1 - s) + 2) * BANK + 256

            for l in range(2):
                g0 = L_SLABS * l
                part = FULL if l == 0 else XPART
                slab(g0, 0, h_hi, h_lo, KD, FULL, 3, SPLITS[f"h{l}"], first=(l == 0))
                slab(g0 + 1, 1, h_hi, h_lo, KD, part, 3, first=(l == 0))
                with pe.Fori(1, 3) as j:
                    for s in range(2):
                        def four(k):
                            if k == 2:
                                pe.wait_ge(evac_done, j * 2 + (g0 + s))
                            if k in (2, 6):
                                pe.wait_ge(modring_in[k // 4], j * 32 + (16 * s - 16))
                                modulation(bass.ds(j * 8 + (beyond(s) + 4 * s + 2 * (k // 4) - 8), 2), modring[:, k // 4, :])

                        slab(j * 2 + (g0 + s), s, h_hi, h_lo, KD, (FULL, part)[s], 3, between=four if l == 0 else None)
                pe.wait_ge(tab_in, 48 * (l + 1))
                with pe.Fori(0, 3) as j:
                    for s in range(2):
                        slab(j * 2 + (g0 + 6 + s), s, h_hi, h_lo, KD, (FULL, part)[s], 3)
                        pe.wait_ge(rope_done, j * 2 + (6 * l + s + 1))
                        for half in range(2):
                            last = T.matmul(ps[:, (6 + half) * BANK:(7 + half) * BANK], ret_const[:, 0, :],
                                            QK[:, bass.ds(j * 2 + s, 1), CTX + 512 * half:CTX + 512 * (half + 1)],
                                            start=True, stop=True)
                        last.then_inc(rot_ready, 1)
                pe.wait_ge(rope_done, 6 * (l + 1) + 1)
                pe.wait_ge(evac_done, g0 + 12)

                def transpose_values(first_unit):
                    u = first_unit
                    for c in range(3):
                        for n0, cnt in GROUPS:
                            if u >= 2:
                                pe.wait_ge(vt_used, u - 1)
                            for t in range(cnt):
                                last = T.transpose(ps[:, (6 + u % 2) * BANK + t * P:(6 + u % 2) * BANK + (t + 1) * P],
                                                   VT[:, c, (n0 + t) * P:(n0 + t + 1) * P], ident)
                            last.then_inc(vt_ready, 1)
                            u += 1

                transpose_values(18 * l)
                pe.wait_ge(vt_used, 18 * l + 9)
                ku = 9 * l

                def turn_pair_keys(p, gi):
                    n0, cnt = GROUPS[gi]
                    u = ku + 3 * p + gi
                    if u >= 2:
                        pe.wait_ge(kt_used, u - 1)
                    if gi == 0 and (p or l):
                        pe.wait_ge(sd_ready, o_groups(l, p))
                    for t in range(cnt):
                        b = (6 + u % 2) * BANK + t * P
                        last = T.transpose(ps[:, b:b + P], QK[:, p, (n0 + t) * P:(n0 + t + 1) * P], ident)
                    last.then_inc(kt_ready, 1)

                def own_scores(p, i):
                    n0, cnt = OUT_TILES[l][i]
                    if i:
                        pe.wait_ge(sd_ready, o_groups(l, p) + i)
                    for a in range(2):
                        r = slice(HD * a, HD * (a + 1))
                        for t in range(cnt):
                            n = n0 + t
                            b = (6 + a) * BANK + t * P
                            last = T.matmul(ps[:, b:b + P], QK[r, p, n * P:(n + 1) * P],
                                            QK[r, 3 + p, n * P:(n + 1) * P], start=True, stop=True)
                    last.then_inc(sc_ready, 1)

                def outputs(p, i):
                    n0, cnt = OUT_TILES[l][i]
                    q = o_groups(l, p) + i
                    pe.wait_ge(state_ready, 3 * l + p + 1)
                    pe.wait_ge(sd_ready, q + 1)
                    pe.wait_ge(qw_ready, q + 1)
                    if i == 2:
                        pe.wait_ge(o_used, q - 1)
                    for t in range(cnt):
                        n = n0 + t
                        c = (i % 2) * BANK + t * P
                        terms = [d for d in range(2) if (d, n) not in ((0, 0), (1, NC - 1))]
                        for x, d in enumerate(terms):
                            T.matmul(ps[:, c:c + P], ST[:, d, STATE_AT[d](n), :], qw[i % 2][:, d, t * P:(t + 1) * P],
                                     start=(x == 0), stop=False, skip_group_check=True)
                        for a in range(2):
                            last = T.matmul(ps[HD * a:HD * (a + 1), c:c + P],
                                            Vt[:, n, p * P + HD * a:p * P + HD * (a + 1)],
                                            SD[i % 2][:, a, t * P:(t + 1) * P], start=False, stop=(a == 1),
                                            skip_group_check=True)
                    last.then_inc(o_ready, 1)

                for gi in range(3):
                    turn_pair_keys(0, gi)
                for p in range(PAIRS):
                    pe.wait_ge(kt_used, ku + 3 * p + 3)
                    own_scores(p, 0)
                    if p or l:
                        pe.wait_ge(o_used, o_groups(l, p))
                    for d in range(2):
                        for x, n in enumerate(BACK if d else range(NT - 1)):
                            b = 3 * d * BANK + x * P
                            last = T.matmul(ps[:, b:b + P], kw[:, d, n, :], Vt[:, n, p * P:(p + 1) * P],
                                            start=True, stop=True)
                        last.then_inc(u_ready, 1)
                    own_scores(p, 1)
                    outputs(p, 0)
                    own_scores(p, 2)
                    outputs(p, 1)
                    if p < PAIRS - 1:
                        turn_pair_keys(p + 1, 0)
                        turn_pair_keys(p + 1, 1)
                    outputs(p, 2)
                    if p < PAIRS - 1:
                        turn_pair_keys(p + 1, 2)
                pe.wait_ge(o_used, o_groups(l, PAIRS))
                hsegs = HN_SEGS[l]
                nu = len(hsegs)
                with pe.Fori(0, PAIRS) as j:
                    for s in range(2):
                        def norms(k):
                            for u, (c0, size) in enumerate(hsegs):
                                c = j * nu + (9 * l + u)
                                if 8 * s + k == HN_AT[l][u]:
                                    T.matmul(ps[:, 6 * BANK:6 * BANK + size], blk, QK[:, bass.ds(j + 3, 1), c0:c0 + size],
                                             start=True, stop=True).then_inc(hn_mean, 1)
                                if 8 * s + k == HN_AT[l][u] + 3:
                                    pe.wait_ge(hn_sq, c + 1)
                                    T.matmul(ps[:, 7 * BANK:7 * BANK + size], blk, hn_tmp[:, 0, c0:c0 + size],
                                             start=True, stop=True).then_inc(hn_var, 1)

                        slab(j * 2 + (g0 + G_NA + s), s, h_hi, h_lo, KD, FULL, 3, between=norms)
                slab(g0 + G_NA + 6, 0, h_hi, h_lo, KD, part, 3)
                pe.wait_ge(evac_done, g0 + G_NA + 6)
                transpose_values(18 * l + 9)
                slab(g0 + G_NA + 7, 1, h_hi, h_lo, KD, part, 3)
                with pe.Fori(1, 3) as j:
                    for s in range(2):
                        slab(j * 2 + (g0 + G_NA + 6 + s), s, h_hi, h_lo, KD, part, 3)
                pe.wait_ge(evac_done, g0 + G_NA + 12)
                tiles = QT + (NC if l == 0 else 0)
                per = 2 * tiles
                ub = 0 if l == 0 else 3 * 2 * (QT + NC)
                with pe.Fori(0, PAIRS) as j:
                    def scores(i):
                        u = j * per + (ub + i)
                        s, (t, a) = i % 2, divmod(i, 2)
                        pe.wait_ge(qz_ready, u + 1)
                        if i >= 2:
                            pe.wait_ge(p_ready, u - 1)
                        rows = QZ[:, t % 2, a, :]
                        o = 2 * s * BANK
                        if t < QT:
                            k0 = CTX + min(max(t - 2, 0), QT - KEYT) * P
                            T.matmul(ps[:, o:o + 512], rows, QK[:, bass.ds(j, 1), k0:k0 + 512], start=True, stop=True)
                            T.matmul(ps[:, o + 512:o + LOC], rows, QK[:, bass.ds(j, 1), k0 + 512:k0 + LOC],
                                     start=True, stop=True)
                        T.matmul(ps[:, o + LOC:o + KEYS], rows, QK[:, bass.ds(j, 1), 0:CTX], start=True, stop=True)\
                            .then_inc(s_ready, 1)

                    def turn_keys(i):
                        u = j * per + (ub + i)
                        s, (t, a) = i % 2, divmod(i, 2)
                        first = 0 if t < QT else KEYT
                        pe.wait_ge(p_ready, u + 1)
                        lu = j * (2 * QT) + (6 * QT * l + min(i, 2 * QT))
                        if i:
                            pe.wait_ge(pt_dve, lu)
                            pe.wait_ge(pt_act, u)
                        for x in range(first, KEYT + NC):
                            last = T.transpose(ps[:, 4 * BANK + x * P:4 * BANK + (x + 1) * P], Sb[s][:, x * P:(x + 1) * P],
                                               ident)
                        last.then_inc(pt_ready, 1)

                    def apply(i):
                        u = j * per + (ub + i)
                        t, a = divmod(i, 2)
                        first = 0 if t < QT else KEYT
                        if t < QT:
                            pe.wait_ge(pt_dve, j * (2 * QT) + (6 * QT * l + i + 1))
                        pe.wait_ge(pt_act, u + 1)
                        if i:
                            pe.wait_ge(os_ready, u)
                        k0 = NC + min(max(t - 2, 0), QT - KEYT)
                        for x in range(first, KEYT + NC):
                            n = k0 + x if x < KEYT else x - KEYT
                            last = T.matmul(ps[:, 6 * BANK:6 * BANK + HD], PT[:, x * P:(x + 1) * P],
                                            Vt[:, n, bass.ds(j * P + HD * a, HD)], start=(x == first),
                                            stop=(x == KEYT + NC - 1))
                        last.then_inc(pv_ready, 1)

                    def turn(t):
                        n = j * tiles + (ub // 2 + t)
                        pe.wait_ge(os_ready, j * per + (ub + 2 * t + 2))
                        if t:
                            pe.wait_ge(ot_used, n)
                        T.transpose(ps[:, 7 * BANK:7 * BANK + P], OS[:, t % 2, :], ident).then_inc(ot_ready, 1)

                    scores(0)
                    scores(1)
                    for i in range(per):
                        turn_keys(i)
                        if i + 2 < per:
                            scores(i + 2)
                        if i >= 3 and i % 2:
                            turn(i // 2 - 1)
                        apply(i)
                    turn(tiles - 1)
                pe.wait_ge(ot_used, ub // 2 + PAIRS * tiles)
                with pe.Fori(0, 4) as j:
                    for s in range(2):
                        def three(k):
                            if k == 1:
                                pe.wait_ge(evac_done, j * 2 + (g0 + G_CONV + s))
                            if k in (1, 3, 5):
                                q = 3 * s + k // 2
                                pe.wait_ge(mod_in[q], j * 16 + 32)
                                modulation(bass.ds(j * 12 + (beyond(s) + 2 * q), 2), modring6[:, q, :])

                        slab(j * 2 + (g0 + G_CONV + s), s, h_hi, h_lo, KD, part, 3, between=three if l == 0 else None)
                segs = FULL if l == 0 else XONLY
                gemm(g0 + G_OUT, 8, h_hi, h_lo, segs, 3, SPLITS[f"y{l}"])
                pe.wait_ge(evac_done, g0 + L_SLABS)
                pe.wait_ge(y_added, l + 1)
                for t0, c0, size in segs:
                    last = T.matmul(ps[:, c0:c0 + size], ones, y_sum[:, t0:t0 + size], start=True, stop=True)
                last.then_inc(stat_ready, 1)
                for k in range(KD):
                    pe.wait_ge(stat_sq, 8 * l + k + 1)
                    for t0, c0, size in segs:
                        last = T.matmul(ps[:, 3 * BANK + c0:3 * BANK + c0 + size], ones, stage[:, k % 2, t0:t0 + size],
                                        start=(k == 0), stop=(k == KD - 1))
                    last.then_inc(stat_used, 1)
                pe.wait_ge(std_ready, l + 1)

            def sumsq(base_k):
                for k in range(KD):
                    sq = T2[:, k % 2, :] if base_k == 16 else C2[:, 8 + k, :]
                    pe.wait_ge(stat_sq, {16: 16, 25: 32, 34: 48}[base_k] + k + 1)
                    for t0, c0, size in SEC:
                        last = T.matmul(ps[:, 4 * BANK + c0:4 * BANK + c0 + size], ones, sq[:, t0:t0 + size],
                                        start=(k == 0), stop=(k == KD - 1))
                    last.then_inc(stat_used, 1)

            def sumsq_added(m, total):
                pe.wait_ge(sq_added, m)
                for t0, c0, size in SEC:
                    last = T.matmul(ps[:, 4 * BANK + c0:4 * BANK + c0 + size], ones, total[:, t0:t0 + size],
                                    start=True, stop=True)
                last.then_inc(stat_used, 1)

            sumsq(16)
            for c in range(8):
                slab(G_RNN + 2 * c, 0, g_hi, g_lo, KD, SEC, 2, SPLITS["h2"] if c == 0 else None)
                slab(G_RNN + 2 * c + 1, 1, g_hi, g_lo, KD, SEC, 2)
                pe.wait_ge(tab_in, 112)
                pe.wait_ge(rnn_xc, c + 1)
                if c:
                    pe.wait_ge(rnn_act, c)
                for m in range(2):
                    for t0, c0, size in SEC:
                        last = T.matmul(ps[:, (4 + 2 * m) * BANK + c0:(4 + 2 * m) * BANK + c0 + size],
                                        rgwt[:, 8 * m + c, :], xcs[c % 2][:, t0:t0 + size], start=True, stop=True)
                last.then_inc(rnn_gates, 1)
            for k in range(KD):
                slab(G_RMIX + 2 * k, 0, g_hi, g_lo, KD, SEC, 2)
                slab(G_RMIX + 2 * k + 1, 1, r_hi, r_lo, KD, SEC, 2, SPLITS["rnn"] if k == 0 else None)
            for c in range(5):
                if c < 4:
                    slab(G_POOL + c, c % 2, g_hi, g_lo, KD, SEC, 2)
                if c:
                    pe.wait_ge(pool_d, c)
                    if c > 1:
                        pe.wait_ge(sp_hi, SPLITS["pool"] + c - 1)
                    for t0, c0, size in SEC:
                        last = T.matmul(ps[:, 4 * BANK + c0:4 * BANK + c0 + size], C2[:, 15, (c - 1) * P:c * P],
                                        C2[:, 12, t0:t0 + size], start=True, stop=True)
                    last.then_inc(pool_ps, 1)
            for k in range(KD):
                slab(G_PMIX + 2 * k, 0, g_hi, g_lo, KD, SEC, 2)
                slab(G_PMIX + 2 * k + 1, 1, r_hi, r_lo, 4, SEC, 2, SPLITS["pool"] if k == 0 else None)
            gemm(G_WO, 8, g_hi, g_lo, SEC, 2, SPLITS["merged"])
            sumsq_added(1, C2[:, 8, :])
            sumsq(25)
            for f in range(FF_GROUPS):
                gf = G_FFN + 24 * f
                gemm(gf, 16, g_hi, g_lo, SEC, 2, SPLITS["h3"])
                gemm(gf + 16, 8, r_hi, r_lo, SEC, 2, SPLITS[f"hid{f}"])
            sumsq_added(2, sq_g[:, 0, :])
            sumsq(34)
            for n in range(8):
                slab(G_PLEP + n, n % 2, p_hi, p_lo, 2, SEC, 2, SPLITS["p"] if n == 0 else None)
            gemm(G_PLEG, 2, g_hi, g_lo, SEC, 2, SPLITS["h4"])
            sumsq_added(3, C2[:, 8, :])
            with pe.Fori(1, 4) as j:
                for s in range(2):
                    slab(j * 2 + (G_PLEG + s), s, g_hi, g_lo, KD, SEC, 2)

        def xcols(l):
            return slice(0 if l == 0 else CTX, T1)

        @block.scalar
        def _(act):
            own = Chain(act, act_step)

            def evac(g, dst, width, slot, func=ACT.Copy, scale=1.0, skip=0):
                act.wait_ge(slab_done, g + 1)
                o = (g % 2) * slot * BANK + skip
                A.activation(dst, ps[:, o:o + width], func, scale=scale).then_inc(evac_done, 1)

            def highs(name, n, src, hi, ready):
                for k in range(n):
                    ready(k)
                    A.activation(hi(k), src(k), ACT.Copy).then_inc(sp_hi, 1)

            def tmp_ready(name):
                return lambda k: act.wait_ge(sp_tmp, TEMPS[name] + k + 1)

            act.dma_start(cm[:], mats).then_inc(const_in, 16)
            act.dma_start(vec[:], vecs).then_inc(const_in, 16)
            act.dma_start(cact[:, 0, :], cT).then_inc(const_in, 16)
            for i in range(1, 8, 2):
                act.dma_start(modfirst[:, 2 * i:2 * i + 2, :], modw[2 * i:2 * i + 2].rearrange("a p n -> p a n"))\
                    .then_inc(mod_in[i], 16)
            for i in range(1, 4, 2):
                act.dma_start(Y[:, 2 * i:2 * i + 2, :], xT[2 * i:2 * i + 2].rearrange("k p t -> p k t"))\
                    .then_inc(x_in[i], 16)
            act.wait_ge(const_in, 48)
            own.link(A.activation(cact[:, 1, :], cact[:, 0, :], ACT.Sigmoid))
            act.wait_ge(lg_ready, 1)
            A.activation(lgt[:, 2, :], lgt[:, 0, :], ACT.Exp, scale=-1.0).then_inc(lg_ready, 1)
            highs("h0", KD, lambda k: stage[:, k % 3, :], lambda k: h_hi[:, k, :], tmp_ready("h0"))

            for l in range(2):
                g0 = L_SLABS * l
                act.wait_ge(sp_lo, SPLITS[f"h{l}"] + 8)
                act.dma_start(cosT[:], ropes[0]).then_inc(tab_in, 16)
                act.dma_start(sinT[:], ropes[1]).then_inc(tab_in, 16)
                act.dma_start(ret_const[:], rets).then_inc(tab_in, 16)
                if l:
                    act.wait_ge(xs_out, 16)
                skip = 0 if l == 0 else CTX

                def evac_part(g, dst, func=ACT.Copy, scale=1.0):
                    evac(g, dst[:, skip:], T1 - skip, 3, func, scale, skip)

                def load_gate(m):
                    if l == 0 and m < 8:
                        if m >= 2:
                            act.wait_ge(mod_used, MOD_FIRST + m - 1)
                        act.dma_start(modring[:, m % 2, :], modw[MOD_FIRST + m]).then_inc(modring_in[m % 2], 16)

                load_gate(0)
                load_gate(1)
                for c in range(3):
                    for s in range(2):
                        if c:
                            load_gate(4 * c + 2 * s - 2)
                            load_gate(4 * c + 2 * s - 1)
                        if s == 0:
                            evac(g0 + 2 * c, QK[:, c, :], T1, 3, scale=HD ** -0.5)
                        else:
                            evac_part(g0 + 2 * c + 1, QK[:, 3 + c, :])
                for c in range(3):
                    evac(g0 + 6 + 2 * c, VT[:, c, :], T1, 3)
                    evac_part(g0 + 7 + 2 * c, Y[:, 2 + c, :], ACT.Silu)

                def evac_values(first_unit):
                    for u in range(9):
                        c, (n0, cnt) = u // 3, GROUPS[u % 3]
                        uu = first_unit + u
                        act.wait_ge(vt_ready, uu + 1)
                        b = (6 + uu % 2) * BANK
                        A.activation(Vt[:, n0:n0 + cnt, c * P:(c + 1) * P],
                                     ps[:, b:b + cnt * P].rearrange("p (t f) -> p t f", f=P), ACT.Copy)\
                            .then_inc(vt_used, 1)

                act.wait_ge(dtab, l + 1)
                lgl = lg[:, 18 * l:18 * l + 18]
                A.activation(Dm[:], dtmp[:], ACT.Exp)
                for d in range(2):
                    for p in range(PAIRS):
                        c = 12 + 3 * d + p
                        A.activation(WQ[:, d, p, :], ret_const[:, 3 + d, :], ACT.Exp, scale=lgl[:, c:c + 1])
                own.link(A.activation(wk[:], wk[:], ACT.Exp))
                A.activation(gch[:], lgl[:, 12:18], ACT.Exp, scale=float(P)).then_inc(wtab, 1)
                evac_values(18 * l)
                for p in range(PAIRS):
                    for i, (n0, cnt) in enumerate(OUT_TILES[l]):
                        act.wait_ge(o_ready, o_groups(l, p) + i + 1)
                        b = (i % 2) * BANK
                        A.activation(QK[:, 3 + p, n0 * P:(n0 + cnt) * P], ps[:, b:b + cnt * P], ACT.Copy).then_inc(o_used, 1)
                ga = g0 + G_NA
                nu = len(HN_SEGS[l])
                with act.Fori(0, PAIRS) as j:
                    def taken(s, dst):
                        act.wait_ge(slab_done, j * 2 + (ga + s + 1))
                        o = s * 3 * BANK
                        A.activation(dst[:, bass.ds(j, 1), :].rearrange("p a n -> p (a n)"), ps[:, o:o + T1], ACT.Copy)\
                            .then_inc(evac_done, 1)

                    for u, (c0, size) in enumerate(HN_SEGS[l]):
                        c = j * nu + (9 * l + u)
                        if HN_AT[l][u] == 8:
                            taken(0, QK)
                        act.wait_ge(hn_diff, c + 1)
                        A.activation(hn_tmp[:, 0, c0:c0 + size],
                                     QK[:, bass.ds(j + 3, 1), c0:c0 + size].rearrange("p a n -> p (a n)"), ACT.Square)\
                            .then_inc(hn_sq, 1)
                        if HN_AT[l][u] == 6:
                            taken(0, QK)
                        act.wait_ge(hn_var, c + 1)
                        A.activation(hn_tmp[:, 1, c0:c0 + size], ps[:, 7 * BANK:7 * BANK + size], ACT.Sqrt,
                                     bias=vcol("eps", 0)).then_inc(hn_std, 1)
                    taken(1, VT)
                def load_bias(j, t):
                    act.dma_start(biasb[:, t % 2, :, :],
                                  bias[bass.ds(j * QT + (PAIRS * QT * l + t), 1)].rearrange("u p a n -> p (u a) n"))\
                        .then_inc(bias_in[t % 2], 16)

                act.wait_ge(hn_done, (9, 15)[l])
                load_bias(0, 0)
                load_bias(0, 1)
                for c in range(3):
                    evac_part(ga + 6 + 2 * c, QK[:, 3 + c, :], scale=HD ** -0.5)
                    if c == 0:
                        evac_values(18 * l + 9)
                    evac_part(ga + 7 + 2 * c, Y[:, 5 + c, :], ACT.Silu)
                tiles = QT + (NC if l == 0 else 0)
                per = 2 * tiles
                ub = 0 if l == 0 else 3 * 2 * (QT + NC)
                act.wait_ge(qz_clear, l + 1)

                def query(j, i):
                    u = j * per + (ub + i)
                    t, a = divmod(i, 2)
                    c0 = CTX + t * P if t < QT else (t - QT) * P
                    if not isinstance(j, int) or PAIRS * per * l + j * per + i >= 4:
                        act.wait_ge(s_ready, u - 3)
                    r = slice(HD * a, HD * (a + 1))
                    A.activation(QZ[r, t % 2, a, :], QK[r, bass.ds(j + 3, 1), c0:c0 + P], ACT.Copy)\
                        .then_inc(qz_ready, 1)

                def pair(j, more):
                    def exps(i):
                        u = j * per + (ub + i)
                        s, t = i % 2, i // 2
                        act.wait_ge(nm_ready, u + 1)
                        o = 2 * s * BANK
                        if t < QT:
                            A.activation(Sb[s][:, :LOC], Sb[s][:, :LOC], ACT.Exp, bias=st[:, s, 2:3],
                                         accum_out=st[:, s, 3:4])
                        A.activation(Sb[s][:, LOC:], ps[:, o + LOC:o + KEYS], ACT.Exp, bias=st[:, s, 2:3],
                                     accum_out=st[:, s, 4:5]).then_inc(p_ready, 1)

                    def rest(i):
                        u = j * per + (ub + i)
                        c0 = 512 if i < 2 * QT else LOC
                        act.wait_ge(pt_ready, u + 1)
                        A.activation(PT[:, c0:KEYS], ps[:, 4 * BANK + c0:4 * BANK + KEYS], ACT.Copy).then_inc(pt_act, 1)

                    def output(i):
                        u = j * per + (ub + i)
                        s, (t, a) = i % 2, divmod(i, 2)
                        act.wait_ge(rinv_ready, u + 1)
                        act.wait_ge(pv_ready, u + 1)
                        if t >= 2:
                            act.wait_ge(ot_ready, j * tiles + (ub // 2 + t - 1))
                        A.activation(OS[:, t % 2, HD * a:HD * (a + 1)], ps[:, 6 * BANK:6 * BANK + HD], ACT.Copy,
                                     scale=st[:, s, 6:7]).then_inc(os_ready, 1)

                    exps(0)
                    act.wait_ge(nm_ready, j * per + (ub + 2))
                    load_bias(j, 2)
                    for i in range(per):
                        rest(i)
                        if i + 4 < per:
                            query(j, i + 4)
                        elif more:
                            query(j + 1, i + 4 - per)
                        if i + 1 < per:
                            exps(i + 1)
                        output(i)
                        if i % 2 and i // 2 + 3 < QT:
                            act.wait_ge(nm_ready, j * per + (ub + i + 3))
                            load_bias(j, i // 2 + 3)
                        if more and i == 2 * QT - 2:
                            load_bias(j + 1, 0)
                            load_bias(j + 1, 1)

                for i in range(4):
                    query(0, i)
                with act.Fori(0, PAIRS - 1) as j:
                    pair(j, True)
                pair(PAIRS - 1, False)
                def load_second(m):
                    if l == 0 and m < 24:
                        if m >= 6:
                            act.wait_ge(mod_used, MOD_FIRST + 8 + m - 5)
                        act.dma_start(modring6[:, m % 6, :], modw[MOD_FIRST + 8 + m]).then_inc(mod_in[m % 6], 16)

                for m in range(6):
                    load_second(m)
                for c in range(2):
                    if c:
                        act.wait_ge(conv_done, 2 * l + 1)
                    for m in range(4):
                        for x in range(3):
                            load_second(6 + 12 * c + 3 * m + x)
                        evac_part(g0 + G_CONV + 4 * c + m, ev[:, m, :], ACT.Silu if m == 3 else ACT.Copy)
                act.wait_ge(conv_done, 2 * l + 2)
                act.dma_start(xin[:], (xT if l == 0 else x_saved).rearrange("k p t -> p k t")).then_inc(xr_in, 16)
                cs = xcols(l)
                highs(f"y{l}", KD, lambda k: Y[:, k, cs], lambda k: h_hi[:, k, cs], lambda k: None)
                for n in range(KD):
                    g = g0 + G_OUT + n
                    act.wait_ge(slab_done, g + 1)
                    if n >= 2:
                        act.wait_ge(xn_ready, 8 * l + n - 1)
                    o = (g % 2) * 3 * BANK
                    gate = 24 * l + 16 + n
                    if l == 0:
                        A.activation(stage[:, n % 2, :CTX], ps[:, o:o + CTX], ACT.Copy, scale=mod[:, gate, 1:2])
                        o += CTX
                    A.activation(stage[:, n % 2, CTX:], ps[:, o:o + SEQ], ACT.Copy, scale=mod[:, gate, 0:1])\
                        .then_inc(evac_done, 1)
                act.wait_ge(xn_ready, 8 * l + 8)
                for k in range(KD):
                    act.wait_ge(diff_ready, 8 * l + k + 1)
                    if k >= 2:
                        act.wait_ge(stat_used, 8 * l + k - 1)
                    A.activation(stage[:, k % 2, cs], Y[:, k, cs], ACT.Square).then_inc(stat_sq, 1)
                act.wait_ge(stat_used, 8 * l + 8)
                A.activation(stage[:, 2, cs], ps[:, 3 * BANK:3 * BANK + T1 - cs.start], ACT.Sqrt, bias=vcol("eps", 0))\
                    .then_inc(std_ready, 1)
                if l == 0:
                    for k in range(KD):
                        act.wait_ge(sp_tmp, TEMPS["h1"] + k + 1)
                        A.activation(h_hi[:, k, :], xin[:, k, :], ACT.Copy).then_inc(sp_hi, 1)
                        own.link(A.activation(Y[:, k, :], Y[:, k, :], ACT.Identity, scale=vcol("lng0", k),
                                              bias=vcol("lnb0", k)))
                    act.dma_start(x_saved.rearrange("k p t -> p k t"), Y[:]).then_inc(xs_out, 16)

            def squares(base_k, src, ready):
                for k in range(KD):
                    ready(k)
                    if base_k == 16:
                        if k >= 2:
                            act.wait_ge(stat_used, base_k + k - 1)
                        dst = T2[:, k % 2, :]
                    else:
                        dst = C2[:, 8 + k, :]
                    A.activation(dst, src(k), ACT.Square).then_inc(stat_sq, 1)

            def square(k, src, sq=C2[:, 8:, :]):
                A.activation(sq[:, k, :], src, ACT.Square).then_inc(stat_sq, 1)

            def std(used, dst):
                act.wait_ge(stat_used, used)
                A.activation(dst, ps[:, 4 * BANK:6 * BANK], ACT.Sqrt, bias=vcol("eps", 1)).then_inc(std_ready, 1)

            squares(16, lambda k: Y[:, k, CTX:], lambda k: act.wait_ge(xn_ready, 16 + k + 1))
            act.dma_start(x_saved.rearrange("k p t -> p k t")[:, :, CTX:], Y[:, :, CTX:]).then_inc(xs_out, 16)
            std(24, T2[:, 2, :])
            highs("h2", KD, lambda k: C2[:, 8 + k, :], lambda k: g_hi[:, k, :], tmp_ready("h2"))
            act.dma_start(rgwt[:], rgw.rearrange("g p n -> p g n")).then_inc(tab_in, 16)
            act.wait_ge(xs_out, 32)

            def rnn_high(c):
                act.wait_ge(sp_tmp, TEMPS["rnn"] + c + 1)
                A.activation(r_hi[:, c, :], B2[:, 6, :], ACT.Copy).then_inc(sp_hi, 1)

            for c in range(8):
                if c:
                    act.wait_ge(rnn_xc, c)
                evac(G_RNN + 2 * c, xb[:, 3:], SEQ, 2)
                if c:
                    rnn_high(c - 1)
                evac(G_RNN + 2 * c + 1, B2[:, 1, :], SEQ, 2, ACT.Gelu_apprx_tanh)
                act.wait_ge(rnn_gates, c + 1)
                own.link(A.activation(B2[:, 2, :], ps[:, 4 * BANK:6 * BANK], ACT.Sigmoid, bias=vcol("b_gates", c)))
                A.activation(B2[:, 3, :], ps[:, 6 * BANK:8 * BANK], ACT.Sigmoid, bias=vcol("b_gates", 8 + c))\
                    .then_inc(rnn_act, 1)
                A.activation(B2[:, 4, :], B2[:, 2, :], ACT.Exp, scale=lru_c[:, 0, c:c + 1])
                A.activation(B2[:, 5, :], B2[:, 2, :], ACT.Tanh, scale=lru_c[:, 1, c:c + 1]).then_inc(rnn_m2, 1)
                act.wait_ge(rnn_mult, 2 * c + 1)
                A.activation(B2[:, 7, :], B2[:, 6, :], ACT.Sqrt).then_inc(rnn_mult, 1)
            rnn_high(7)

            def mix(g0, first):
                for n in range(KD):
                    if n + first >= 2:
                        act.wait_ge(mix_used, first + n - 1)
                    evac(g0 + 2 * n, T2[:, n % 2, :], SEQ, 2, ACT.Sigmoid)
                    evac(g0 + 2 * n + 1, T2[:, 2 + n % 2, :], SEQ, 2)

            mix(G_RMIX, 0)
            act.wait_ge(slab_done, G_POOL)
            act.dma_start(C2[:, 15, :4 * P], poolw.rearrange("g p n -> p g n")).then_inc(tab_in, 16)
            act.dma_start(C2[:, 14, :64], pooltab).then_inc(tab_in, 16)
            for c in range(5):
                if c < 4:
                    if c:
                        act.wait_ge(pool_d, c)
                    evac(G_POOL + c, pu[:, 16:], SEQ, 2)
                if c:
                    act.wait_ge(pool_ps, c)
                    if c > 1:
                        act.wait_ge(sp_lo, SPLITS["pool"] + c - 1)
                    own.link(A.activation(C2[:, 13, :], ps[:, 4 * BANK:6 * BANK], ACT.Copy, scale=vcol("pool_scale", c - 1)))
                    A.activation(r_hi[:, c - 1, :], C2[:, 13, :], ACT.Copy).then_inc(sp_hi, 1)
            mix(G_PMIX, 8)
            act.wait_ge(slab_done, G_WO)
            highs("merged", KD, lambda k: B2[:, k, :], lambda k: g_hi[:, k, :],
                  lambda k: act.wait_ge(mix_used, 8 + k + 1))
            act.wait_ge(sp_lo, SPLITS["merged"] + 8)
            act.dma_start(B2[:], x_saved.rearrange("k p t -> p k t")[:, :, CTX:]).then_inc(xr_in, 16)
            for n in range(KD):
                evac(G_WO + n, C2[:, n, :], SEQ, 2)
                act.wait_ge(evac_done, G_WO + n + 1)
                square(n, C2[:, n, :])
            std(25, T2[:, 2, :])
            squares(32, lambda k: B2[:, k, :], lambda k: act.wait_ge(xn_ready, 24 + k + 1))
            act.dma_start(x_saved.rearrange("k p t -> p k t")[:, :, CTX:], B2[:]).then_inc(xs_out, 16)
            std(33, T2[:, 2, :])
            act.wait_ge(slab_done, G_FFN)
            highs("h3", KD, lambda k: C2[:, k, :], lambda k: g_hi[:, k, :], tmp_ready("h3"))
            act.wait_ge(xs_out, 48)
            for f in range(FF_GROUPS):
                gf = G_FFN + 24 * f
                for c in range(FF_CHUNKS):
                    cc = FF_CHUNKS * f + c
                    if cc:
                        act.wait_ge(ff_conv, cc)
                    evac(gf + 2 * c, gpad[:, 2:], SEQ, 2)
                    act.wait_ge(ff_conv, cc + 1)
                    A.activation(ffc[:], ffc[:], ACT.Gelu_apprx_tanh, bias=vcol("fconvb", cc)).then_inc(ff_gelu, 1)
                    if c == 0 and f > 1:
                        act.wait_ge(acc_used, 8 * (f - 1))
                    evac(gf + 2 * c + 1, ffu[:], SEQ, 2)
                    act.wait_ge(sp_tmp, TEMPS[f"hid{f}"] + c + 1)
                    A.activation(r_hi[:, c, :], fft[:], ACT.Copy).then_inc(sp_hi, 1)
                for n in range(KD):
                    if f == 0:
                        evac(gf + 16 + n, B2[:, n, :], SEQ, 2)
                    else:
                        if n >= 2:
                            act.wait_ge(acc_used, 8 * (f - 1) + n - 1)
                        evac(gf + 16 + n, (ffu, fft)[n % 2][:], SEQ, 2)
                        if f == FF_GROUPS - 1 and n:
                            act.wait_ge(acc_used, 8 * (f - 1) + n)
                            square(n - 1, B2[:, n - 1, :], sq_g)
            act.wait_ge(acc_used, 8 * (FF_GROUPS - 1))
            square(KD - 1, B2[:, KD - 1, :], sq_g)
            act.dma_start(C2[:, 0:8, :], x_saved.rearrange("k p t -> p k t")[:, :, CTX:]).then_inc(xr_in, 16)
            std(34, T2[:, 2, :])
            squares(48, lambda k: B2[:, k, :], lambda k: act.wait_ge(xn_ready, 32 + k + 1))
            act.dma_start(C2[:, 0:2, :], pT.rearrange("k p t -> p k t")).then_inc(tab_in, 16)
            std(42, C2[:, 7, :])
            act.wait_ge(tab_in, 160)
            highs("p", 2, lambda k: C2[:, k, :], lambda k: p_hi[:, k, :], lambda k: None)
            highs("h4", KD, lambda k: C2[:, 8 + k, :], lambda k: g_hi[:, k, :], tmp_ready("h4"))
            for n in range(KD):
                evac(G_PLEP + n, C2[:, n, :], SEQ, 2)
            act.wait_ge(sp_lo, SPLITS["h4"] + 8)
            for n in range(KD):
                act.wait_ge(evac_done, G_PLEP + n + 1)
                square(n, C2[:, n, :])
            for n in range(KD):
                if n == 2:
                    std(43, T2[:, 2, :])
                if n >= 2:
                    act.wait_ge(out_ready, n - 1)
                evac(G_PLEG + n, T2[:, n % 2, :], SEQ, 2, ACT.Sigmoid)

        @block.vector
        def _(dve):
            own = Chain(dve, dve_step)

            def lows(name, n, src, hi, lo, make=None):
                for k in range(n + 1):
                    if 3 <= k < n and make is not None:
                        dve.wait_ge(sp_lo, SPLITS[name] + k - 2)
                    if k < n and make is not None:
                        make(k).then_inc(sp_tmp, 1)
                    if k:
                        dve.wait_ge(sp_hi, SPLITS[name] + k)
                        V.tensor_tensor(lo(k - 1), src(k - 1), hi(k - 1).bitcast(F32), ALU.subtract).then_inc(sp_lo, 1)

            V.memset(pool_zero[:, 1:2], 0.0).then_inc(rope_done, 1)
            dve.wait_ge(const_in, 48)
            lin = vec[:, VEC["dec0"][0]:VEC["dec0"][0] + 44]
            own.link(V.scalar_tensor_tensor(lgt[:, 0, :], lin, -1.0, lin, ALU.mult, ALU.max))
            V.tensor_scalar(lgt[:, 1, :], lin, 0.0, None, ALU.min).then_inc(lg_ready, 1)
            dve.wait_ge(act_step, 1)
            V.tensor_tensor(cact[:, 2, :], cact[:, 0, :], cact[:, 1, :], ALU.mult).then_inc(cact_ready, 1)
            dve.wait_ge(lg_ready, 2)
            own.link(V.tensor_scalar(lgt[:, 3, :], lgt[:, 2, :], 2.0, None, ALU.add))
            own.link(V.reciprocal(lgt[:, 3, :], lgt[:, 3, :]))
            own.link(V.tensor_tensor(lgt[:, 2, :], lgt[:, 2, :], lgt[:, 3, :], ALU.mult))
            own.link(V.tensor_tensor(lgt[:, 3, :], lgt[:, 2, :], lgt[:, 2, :], ALU.mult))
            own.link(V.tensor_scalar(lgt[:, 4, :], lgt[:, 3, :], 1.0 / 17, 1.0 / 15, ALU.mult, ALU.add))
            for m in (13, 11, 9, 7, 5, 3, 1):
                own.link(V.tensor_tensor(lgt[:, 4, :], lgt[:, 4, :], lgt[:, 3, :], ALU.mult))
                own.link(V.tensor_scalar(lgt[:, 4, :], lgt[:, 4, :], 1.0 / m, None, ALU.add))
            own.link(V.scalar_tensor_tensor(lgt[:, 5, :], lgt[:, 2, :], -2.0, lgt[:, 4, :], ALU.mult, ALU.mult))
            own.link(V.tensor_tensor(lg[:], lgt[:, 5, :], lgt[:, 1, :], ALU.add))
            own.link(V.tensor_scalar(lru_c[:, 0, :], lg[:, 36:44], LRU_C, None, ALU.mult))
            own.link(V.tensor_scalar(lru_c[:, 1, :], lg[:, 36:44], -LRU_C, None, ALU.mult))
            dve.wait_ge(mod_used, MOD_FIRST)
            own.link(V.tensor_tensor(mod[:, :MOD_FIRST, :].rearrange("p a b -> p (a b)"),
                                     ps[:, 7 * BANK:7 * BANK + 2 * MOD_FIRST], vcol("bmod", 0, 2 * MOD_FIRST), ALU.add))
            own.link(V.tensor_scalar(mod[:, 8:16, :], mod[:, 8:16, :], 1.0, None, ALU.add))

            def later_modulation(m, turns, n):
                size = turns * 4 * n

                def half(x, s):
                    return x.rearrange("p (g s q) -> p g s q", g=turns, s=2)[:, :, s, :]

                for s in range(2):
                    a = (3 * (1 - s) + 2) * BANK + 256
                    own.link(V.tensor_tensor(half(mod[:, m:m + 2 * turns * n, :].rearrange("p a b -> p (a b)"), s),
                                             half(ps[:, a:a + size], s), half(vcol("bmod", 2 * m, size), s), ALU.add))

            def modulated(l, dst, src, k):
                a, b = 24 * l + 8 + k, 24 * l + k
                V.tensor_scalar(dst[:, :CTX], src[:, :CTX], mod[:, a, 1:2], mod[:, b, 1:2], ALU.mult, ALU.add)
                return V.tensor_scalar(dst[:, CTX:], src[:, CTX:], mod[:, a, 0:1], mod[:, b, 0:1], ALU.mult, ALU.add)

            def modulated_input(k):
                if k % 2 == 0:
                    dve.wait_ge(x_in[k // 2], 16)
                return modulated(0, stage[:, k % 3, :], Y[:, k, :], k)

            lows("h0", KD, lambda k: stage[:, k % 3, :], lambda k: h_hi[:, k, :], lambda k: h_lo[:, k, :],
                 lambda k: modulated_input(k))

            for l in range(2):
                g0 = L_SLABS * l
                lgl = lg[:, 18 * l:18 * l + 18]
                dve.wait_ge(tab_in, 48 * (l + 1))
                for c in range(6):
                    x = QK[:, c, CTX:]
                    dve.wait_ge(rot_ready, 6 * l + c + 1)
                    dve.wait_ge(rope_done, 6 * l + c + 1)
                    own.link(V.tensor_tensor(rope_tmp[:], ps[:, 6 * BANK:8 * BANK], sinT[:], ALU.mult))
                    own.link(V.tensor_tensor(x, x, cosT[:], ALU.mult))
                    V.tensor_tensor(x, x, rope_tmp[:], ALU.add).then_inc(rope_done, 1)
                dve.wait_ge(rope_done, 6 * l + 7)
                if l == 0:
                    dve.wait_ge(mod_used, MOD_FIRST + 8)
                    dve.wait_ge(evac_done, 12)
                    later_modulation(MOD_FIRST, 2, 2)
                for h in range(6):
                    own.link(V.tensor_scalar(dtmp[:, h, :], ret_const[:, 1, :], lgl[:, h:h + 1], None, ALU.mult))
                    own.link(V.scalar_tensor_tensor(dtmp[:, h, :], ret_const[:, 2, :], lgl[:, 6 + h:7 + h], dtmp[:, h, :],
                                                    ALU.mult, ALU.add))
                V.tensor_scalar(wk[:, 0:6], lgl[:, 0:6], vcol("cols", 0), None, ALU.mult)
                V.tensor_scalar(wk[:, 6:12], lgl[:, 6:12], vcol("cols", 1), None, ALU.mult).then_inc(dtab, 1)
                dve.wait_ge(vt_ready, 18 * l + 9)
                own.link(V.memset(ST[:], 0.0))
                dve.wait_ge(wtab, l + 1)
                if l:
                    dve.wait_ge(xs_out, 16)
                for p in range(PAIRS):
                    for gi, (n0, cnt) in enumerate(GROUPS):
                        u = 9 * l + 3 * p + gi
                        dve.wait_ge(kt_ready, u + 1)
                        if gi == 0 and 3 * l + p:
                            dve.wait_ge(u_ready, 2 * (3 * l + p))
                        b = (6 + u % 2) * BANK
                        src = ps[:, b:b + cnt * P].rearrange("p (t f) -> p t f", f=P)
                        for d in range(2):
                            for a in range(2):
                                c = 6 * d + 2 * p + a
                                last = V.tensor_scalar(kw[:, d, n0:n0 + cnt, HD * a:HD * (a + 1)],
                                                       src[:, :, HD * a:HD * (a + 1)], wk[:, c:c + 1], None, ALU.mult)
                        last.then_inc(kt_used, 1)
                    q = o_groups(l, p)

                    def decayed(i):
                        cnt = OUT_TILES[l][i][1]
                        if i != 1 and q + i:
                            dve.wait_ge(o_ready, q + (1 if i else 0))
                        dve.wait_ge(sc_ready, q + i + 1)
                        for a in range(2):
                            b = (6 + a) * BANK
                            last = V.tensor_tensor(SD[i % 2][:, a, :cnt * P].rearrange("p (t f) -> p t f", f=P),
                                                   ps[:, b:b + cnt * P].rearrange("p (t f) -> p t f", f=P),
                                                   Dm[:, 2 * p + a, :].unsqueeze(1).to_broadcast([P, cnt, P]), ALU.mult)
                        last.then_inc(sd_ready, 1)

                    decayed(0)
                    for d in range(2):
                        dve.wait_ge(u_ready, 2 * (3 * l + p) + d + 1)
                        for x in range(NT - 1):
                            for a in range(2):
                                r = slice(HD * a, HD * (a + 1))
                                c = 3 * d * BANK + x * P + HD * a
                                if x == 0:
                                    ins = V.tensor_copy(ST[r, d, 0, r], ps[r, c:c + HD])
                                else:
                                    ins = V.scalar_tensor_tensor(ST[r, d, x, r], ST[r, d, x - 1, r],
                                                                 gch[r, 3 * d + p:3 * d + p + 1], ps[r, c:c + HD],
                                                                 ALU.mult, ALU.add)
                                if x == NT - 2 and d == 1 and a == 1:
                                    ins.then_inc(state_ready, 1)
                                else:
                                    own.step(ins)
                            if x < NT - 2:
                                dve.wait_ge(dve_step, own.n)
                    decayed(1)
                    decayed(2)
                nu = len(HN_SEGS[l])
                with dve.Fori(0, PAIRS) as j:
                    own.enter(j, 2 * nu)
                    for u, (c0, size) in enumerate(HN_SEGS[l]):
                        c = j * nu + (9 * l + u)
                        o = QK[:, bass.ds(j + 3, 1), c0:c0 + size].rearrange("p a n -> p (a n)")
                        y = Y[:, bass.ds(j + 2, 1), c0:c0 + size].rearrange("p a n -> p (a n)")
                        dve.wait_ge(hn_mean, c + 1)
                        V.tensor_tensor(o, o, ps[:, 6 * BANK:6 * BANK + size], ALU.subtract).then_inc(hn_diff, 1)
                        dve.wait_ge(hn_std, c + 1)
                        own.link(V.reciprocal(hn_tmp[:, 1, c0:c0 + size], hn_tmp[:, 1, c0:c0 + size]))
                        own.link(V.tensor_tensor(o, o, hn_tmp[:, 1, c0:c0 + size], ALU.mult))
                        V.tensor_tensor(y, y, o, ALU.mult).then_inc(hn_done, 1)
                own.leave(PAIRS)
                V.memset(QZ[:], 0.0).then_inc(qz_clear, 1)
                tiles = QT + (NC if l == 0 else 0)
                per = 2 * tiles
                ub = 0 if l == 0 else 3 * 2 * (QT + NC)
                locals_ = 2 * QT
                steps_per = locals_ * 3 + (per - locals_)
                with dve.Fori(0, PAIRS) as j:
                    own.enter(j, steps_per)

                    def maxima(i):
                        u = j * per + (ub + i)
                        s, (t, a) = i % 2, divmod(i, 2)
                        o = 2 * s * BANK
                        dve.wait_ge(s_ready, u + 1)
                        if i >= 2:
                            dve.wait_ge(p_ready, u - 1)
                        if t < QT:
                            dve.wait_ge(bias_in[t % 2], j * (16 * QT // 2) + (16 * (3 * QT // 2 * l + t // 2 + 1)))
                        if i >= 2:
                            dve.wait_ge(pt_ready, u - 1)
                        if t < QT:
                            own.step(V.reduce_max(st[:, s, 0:1], ps[:, o + LOC:o + KEYS], AX.X))
                            own.link(V.tensor_tensor_reduce(out=Sb[s][:, :LOC], in0=ps[:, o:o + LOC],
                                                            in1=biasb[:, t % 2, a, :], scale=1.0, scalar=MASKED,
                                                            op0=ALU.add, op1=ALU.max, accum_out=st[:, s, 1:2]))
                            V.tensor_scalar(st[:, s, 2:3], st[:, s, 0:1], st[:, s, 1:2], -1.0, ALU.max, ALU.mult)\
                                .then_inc(nm_ready, 1)
                        else:
                            own.link(V.reduce_max(st[:, s, 0:1], ps[:, o + LOC:o + KEYS], AX.X))
                            V.tensor_scalar(st[:, s, 2:3], st[:, s, 0:1], -1.0, None, ALU.mult).then_inc(nm_ready, 1)

                    def sums(i):
                        u = j * per + (ub + i)
                        s, t = i % 2, i // 2
                        dve.wait_ge(p_ready, u + 1)
                        if i >= 2:
                            dve.wait_ge(os_ready, u - 1)
                        if t < QT:
                            own.link(V.tensor_tensor(st[:, s, 5:6], st[:, s, 3:4], st[:, s, 4:5], ALU.add))
                            V.reciprocal(st[:, s, 6:7], st[:, s, 5:6]).then_inc(rinv_ready, 1)
                            dve.wait_ge(pt_ready, u + 1)
                            V.tensor_copy(PT[:, 0:512], ps[:, 4 * BANK:5 * BANK]).then_inc(pt_dve, 1)
                        else:
                            V.reciprocal(st[:, s, 6:7], st[:, s, 4:5]).then_inc(rinv_ready, 1)

                    def place(t):
                        c0 = CTX + t * P if t < QT else (t - QT) * P
                        dve.wait_ge(ot_ready, j * tiles + (ub // 2 + t + 1))
                        y = Y[:, bass.ds(j + 5, 1), c0:c0 + P].rearrange("p a n -> p (a n)")
                        V.tensor_tensor(y, ps[:, 7 * BANK:7 * BANK + P], y, ALU.mult).then_inc(ot_used, 1)

                    maxima(0)
                    maxima(1)
                    for i in range(per):
                        sums(i)
                        if i >= 4 and i % 2 == 0:
                            place(i // 2 - 2)
                        if i + 2 < per:
                            maxima(i + 2)
                    place(tiles - 2)
                    place(tiles - 1)
                own.leave(PAIRS)
                cs = xcols(l)
                for c in range(2):
                    ge = g0 + G_CONV + 4 * c
                    dve.wait_ge(evac_done, ge + 2)
                    if c == 0:
                        if l == 0:
                            V.memset(convu[:, 0:1], 0.0)
                        V.memset(convu[:, CTX + 1:CTX + 3], 0.0)
                        V.memset(convu[:, T1 + 3:T1 + 4], 0.0)
                    if l == 0:
                        V.tensor_tensor(convu[:, 1:CTX + 1], ev[:, 0, :CTX], ev[:, 1, :CTX], ALU.mult)
                    own.link(V.tensor_tensor(convu[:, CTX + 3:T1 + 3], ev[:, 0, CTX:], ev[:, 1, CTX:], ALU.mult))
                    taps = [vcol(f"convw{l}", 2 * i + c) for i in range(3)]
                    o = 0 if l == 0 else CTX + 2
                    n = T1 + 2 - o
                    co = convo[:, o:]
                    own.link(V.tensor_scalar(co, convu[:, o + 1:o + 1 + n], taps[1], vcol(f"convb{l}", c), ALU.mult, ALU.add))
                    own.link(V.scalar_tensor_tensor(co, convu[:, o:o + n], taps[0], co, ALU.mult, ALU.add))
                    own.link(V.scalar_tensor_tensor(co, convu[:, o + 2:o + 2 + n], taps[2], co, ALU.mult, ALU.add))
                    dve.wait_ge(evac_done, ge + 4)
                    if l == 0:
                        V.tensor_tensor(ev[:, 2, :CTX], ev[:, 2, :CTX], convo[:, :CTX], ALU.mult)
                    own.link(V.tensor_tensor(ev[:, 2, CTX:], ev[:, 2, CTX:], convo[:, CTX + 2:], ALU.mult))
                    V.tensor_tensor(Y[:, c, cs], ev[:, 2, cs], ev[:, 3, cs], ALU.mult).then_inc(conv_done, 1)
                if l == 0:
                    dve.wait_ge(mod_used, MOD_ALL)
                    dve.wait_ge(evac_done, g0 + G_OUT)
                    later_modulation(MOD_FIRST + 8, 4, 3)
                    own.link(V.tensor_scalar(mod[:, 32:40, :], mod[:, 32:40, :], 1.0, None, ALU.add))
                    wide = [vcol(n, 0, 8).unsqueeze(2).to_broadcast([P, 8, 2]) for n in ("lng0", "lnb0")]
                    own.link(V.tensor_tensor(mod_ln[:, 0:8, :], mod[:, 32:40, :], wide[0], ALU.mult))
                    own.link(V.tensor_tensor(mod_ln[:, 8:16, :], mod[:, 32:40, :], wide[1], ALU.mult))
                    own.link(V.tensor_tensor(mod_ln[:, 8:16, :], mod_ln[:, 8:16, :], mod[:, 24:32, :], ALU.add))
                lows(f"y{l}", KD, lambda k: Y[:, k, cs], lambda k: h_hi[:, k, cs], lambda k: h_lo[:, k, cs])
                dve.wait_ge(xr_in, 16 * (l + 1))
                for n in range(KD):
                    dve.wait_ge(evac_done, g0 + G_OUT + n + 1)
                    V.scalar_tensor_tensor(Y[:, n, cs], xin[:, n, cs], ALPHA, stage[:, n % 2, cs], ALU.mult, ALU.add)\
                        .then_inc(xn_ready, 1)
                    if n:
                        dve.wait_ge(xn_ready, 8 * l + n + 1)
                        ins = V.tensor_tensor(y_sum[:, cs], Y[:, 0, cs] if n == 1 else y_sum[:, cs], Y[:, n, cs], ALU.add)
                        if n == KD - 1:
                            ins.then_inc(y_added, 1)
                        else:
                            own.link(ins)
                dve.wait_ge(stat_ready, l + 1)
                for k in range(KD):
                    V.tensor_tensor(Y[:, k, cs], Y[:, k, cs], ps[:, 0:T1 - cs.start], ALU.subtract)\
                        .then_inc(diff_ready, 1)
                dve.wait_ge(std_ready, l + 1)
                own.link(V.reciprocal(stage[:, 2, cs], stage[:, 2, cs]))

                def normed(k):
                    own.link(V.tensor_tensor(Y[:, k, cs], Y[:, k, cs], stage[:, 2, cs], ALU.mult))
                    return V.tensor_scalar(Y[:, k, cs], Y[:, k, cs], vcol(f"lng{l}", k), vcol(f"lnb{l}", k),
                                           ALU.mult, ALU.add)

                def next_input(k):
                    own.link(V.tensor_tensor(Y[:, k, :], Y[:, k, :], stage[:, 2, :], ALU.mult))
                    a, b = mod_ln[:, k, :], mod_ln[:, 8 + k, :]
                    V.tensor_scalar(xin[:, k, :CTX], Y[:, k, :CTX], a[:, 1:2], b[:, 1:2], ALU.mult, ALU.add)
                    return V.tensor_scalar(xin[:, k, CTX:], Y[:, k, CTX:], a[:, 0:1], b[:, 0:1], ALU.mult, ALU.add)

                if l == 0:
                    lows("h1", KD, lambda k: xin[:, k, :], lambda k: h_hi[:, k, :], lambda k: h_lo[:, k, :], next_input)
                else:
                    for k in range(KD):
                        normed(k).then_inc(xn_ready, 1)

            def rsqrt(count, buf):
                dve.wait_ge(std_ready, count)
                own.link(V.reciprocal(buf, buf))

            def add_square(k, first, sq=C2[:, 8:, :]):
                dve.wait_ge(stat_sq, first + k + 1)
                ins = V.tensor_tensor(sq[:, 0, :], sq[:, 0, :], sq[:, k, :], ALU.add)
                if k == KD - 1:
                    ins.then_inc(sq_added, 1)
                else:
                    own.link(ins)

            rs = T2[:, 2, :]
            rsqrt(3, rs)
            lows("h2", KD, lambda k: C2[:, 8 + k, :], lambda k: g_hi[:, k, :], lambda k: g_lo[:, k, :],
                 lambda k: V.scalar_tensor_tensor(C2[:, 8 + k, :], Y[:, k, CTX:], vcol("g_mix_pre", k), rs,
                                                  ALU.mult, ALU.mult))
            dve.wait_ge(xs_out, 32)
            own.link(V.memset(xb[:, 0:3], 0.0))

            def convolved(c):
                xc = xcs[c % 2]
                dve.wait_ge(evac_done, G_RNN + 2 * c + 1)
                tap = lambda i: vcol("rconvw", 8 * i + c)
                own.link(V.tensor_scalar(xc, xb[:, 0:SEQ], tap(0), vcol("rconvb", c), ALU.mult, ALU.add))
                for i in (1, 2):
                    own.link(V.scalar_tensor_tensor(xc, xb[:, i:i + SEQ], tap(i), xc, ALU.mult, ALU.add))
                V.scalar_tensor_tensor(xc, xb[:, 3:], tap(3), xc, ALU.mult, ALU.add).then_inc(rnn_xc, 1)

            def gated_input(c):
                dve.wait_ge(rnn_m2, c + 1)
                dve.wait_ge(rnn_xc, c + 1)
                dve.wait_ge(sp_lo, SPLITS["rnn"] + c)
                own.link(V.tensor_tensor(B2[:, 6, :], B2[:, 4, :], B2[:, 4, :], ALU.mult))
                V.scalar_tensor_tensor(B2[:, 6, :], B2[:, 6, :], 1.0, B2[:, 5, :], ALU.add, ALU.mult).then_inc(rnn_mult, 1)
                own.link(V.tensor_tensor(B2[:, 3, :], B2[:, 3, :], xcs[c % 2], ALU.mult))

            def recurred(c):
                dve.wait_ge(rnn_mult, 2 * c + 2)
                own.link(V.memset(B2[:, 7, 0:1], 1.0))
                own.link(V.tensor_tensor(B2[:, 3, :], B2[:, 3, :], B2[:, 7, :], ALU.mult))
                own.link(V.tensor_tensor_scan(B2[:, 5, :], B2[:, 4, :], B2[:, 3, :], 0.0, ALU.mult, ALU.add))
                dve.wait_ge(evac_done, G_RNN + 2 * c + 2)
                V.tensor_tensor(B2[:, 6, :], B2[:, 5, :], B2[:, 1, :], ALU.mult).then_inc(sp_tmp, 1)
                dve.wait_ge(sp_hi, SPLITS["rnn"] + c + 1)
                V.tensor_tensor(r_lo[:, c, :], B2[:, 6, :], r_hi[:, c, :].bitcast(F32), ALU.subtract).then_inc(sp_lo, 1)

            convolved(0)
            for c in range(8):
                gated_input(c)
                if c < 7:
                    convolved(c + 1)
                recurred(c)
            for n in range(KD):
                dve.wait_ge(evac_done, G_RMIX + 2 * n + 2)
                V.tensor_tensor(B2[:, n, :], T2[:, n % 2, :], T2[:, 2 + n % 2, :], ALU.mult).then_inc(mix_used, 1)
            dve.wait_ge(slab_done, G_POOL)
            for buf in (pu, pa, pb):
                own.link(V.memset(buf[:, 0:16], 0.0))
            dve.wait_ge(tab_in, 144)
            for c in range(4):
                dve.wait_ge(evac_done, G_POOL + c + 1)
                if c:
                    dve.wait_ge(pool_d, c)
                s = pu
                for i in range(c + 1):
                    dst, sh = (pa, pb)[i % 2], 1 << i
                    own.link(V.tensor_tensor(dst[:, 16:], s[:, 16:], s[:, 16 - sh:16 + SEQ - sh], ALU.add))
                    s = dst
                if c:
                    dve.wait_ge(pool_ps, c)
                own.link(V.tensor_tensor(C2[:, 12, :16], s[:, 16:32], C2[:, 14, 16 * c:16 * c + 16], ALU.mult))
                V.tensor_tensor(C2[:, 12, :16], C2[:, 12, :16], pu[:, 16:32], ALU.subtract)
                V.scalar_tensor_tensor(C2[:, 12, 16:], s[:, 32:], 1.0 / (2 << c), pu[:, 32:], ALU.mult, ALU.subtract)\
                    .then_inc(pool_d, 1)
                if c:
                    dve.wait_ge(sp_hi, SPLITS["pool"] + c)
                    V.tensor_tensor(r_lo[:, c - 1, :], C2[:, 13, :], r_hi[:, c - 1, :].bitcast(F32), ALU.subtract)\
                        .then_inc(sp_lo, 1)
            dve.wait_ge(sp_hi, SPLITS["pool"] + 4)
            V.tensor_tensor(r_lo[:, 3, :], C2[:, 13, :], r_hi[:, 3, :].bitcast(F32), ALU.subtract).then_inc(sp_lo, 1)
            for n in range(KD):
                dve.wait_ge(evac_done, G_PMIX + 2 * n + 2)
                own.link(V.tensor_tensor(T2[:, n % 2, :], T2[:, n % 2, :], T2[:, 2 + n % 2, :], ALU.mult))
                V.tensor_tensor(B2[:, n, :], B2[:, n, :], T2[:, n % 2, :], ALU.add).then_inc(mix_used, 1)
            lows("merged", KD, lambda k: B2[:, k, :], lambda k: g_hi[:, k, :], lambda k: g_lo[:, k, :])
            for k in range(1, KD):
                add_square(k, 24)
            dve.wait_ge(xr_in, 48)
            rsqrt(4, rs)
            for k in range(KD):
                own.link(V.scalar_tensor_tensor(C2[:, k, :], C2[:, k, :], vcol("g_mix_post", k), rs, ALU.mult, ALU.mult))
                V.tensor_tensor(B2[:, k, :], B2[:, k, :], C2[:, k, :], ALU.add).then_inc(xn_ready, 1)
            rsqrt(5, rs)
            lows("h3", KD, lambda k: C2[:, k, :], lambda k: g_hi[:, k, :], lambda k: g_lo[:, k, :],
                 lambda k: V.scalar_tensor_tensor(C2[:, k, :], B2[:, k, :], vcol("g_ffn_pre", k), rs, ALU.mult, ALU.mult))
            own.link(V.memset(gpad[:, 0:2], 0.0))
            for f in range(FF_GROUPS):
                gf = G_FFN + 24 * f
                for c in range(FF_CHUNKS):
                    cc = FF_CHUNKS * f + c
                    dve.wait_ge(evac_done, gf + 2 * c + 1)
                    own.link(V.tensor_scalar(ffc[:], gpad[:, 2:], vcol("fconvw", 48 + cc), None, ALU.mult))
                    own.link(V.scalar_tensor_tensor(ffc[:], gpad[:, 1:1 + SEQ], vcol("fconvw", 24 + cc), ffc[:],
                                                    ALU.mult, ALU.add))
                    V.scalar_tensor_tensor(ffc[:], gpad[:, 0:SEQ], vcol("fconvw", cc), ffc[:], ALU.mult, ALU.add)\
                        .then_inc(ff_conv, 1)
                    dve.wait_ge(ff_gelu, cc + 1)
                    dve.wait_ge(evac_done, gf + 2 * c + 2)
                    dve.wait_ge(sp_lo, SPLITS[f"hid{f}"] + c)
                    V.tensor_tensor(fft[:], ffc[:], ffu[:], ALU.mult).then_inc(sp_tmp, 1)
                    dve.wait_ge(sp_hi, SPLITS[f"hid{f}"] + c + 1)
                    V.tensor_tensor(r_lo[:, c, :], fft[:], r_hi[:, c, :].bitcast(F32), ALU.subtract).then_inc(sp_lo, 1)
                if f:
                    for n in range(KD):
                        dve.wait_ge(evac_done, gf + 16 + n + 1)
                        V.tensor_tensor(B2[:, n, :], B2[:, n, :], (ffu, fft)[n % 2][:], ALU.add).then_inc(acc_used, 1)
                        if f == FF_GROUPS - 1 and n >= 2:
                            add_square(n - 1, 40, sq_g)
            add_square(KD - 1, 40, sq_g)
            rsqrt(6, rs)
            dve.wait_ge(xr_in, 64)
            for k in range(KD):
                own.link(V.scalar_tensor_tensor(B2[:, k, :], B2[:, k, :], vcol("g_ffn_post", k), rs, ALU.mult, ALU.mult))
                V.tensor_tensor(B2[:, k, :], B2[:, k, :], C2[:, k, :], ALU.add).then_inc(xn_ready, 1)
            rs2 = C2[:, 7, :]
            rsqrt(7, rs2)
            lows("p", 2, lambda k: C2[:, k, :], lambda k: p_hi[:, k, :], lambda k: p_lo[:, k, :])
            lows("h4", KD, lambda k: C2[:, 8 + k, :], lambda k: g_hi[:, k, :], lambda k: g_lo[:, k, :],
                 lambda k: V.scalar_tensor_tensor(C2[:, 8 + k, :], B2[:, k, :], vcol("g_ple_gate", k), rs2,
                                                  ALU.mult, ALU.mult))
            for k in range(1, KD):
                add_square(k, 56)
            rsqrt(8, rs)
            for n in range(KD):
                own.link(V.scalar_tensor_tensor(C2[:, n, :], C2[:, n, :], vcol("g_ple_post", n), rs, ALU.mult, ALU.mult))
                dve.wait_ge(evac_done, G_PLEG + n + 1)
                own.link(V.tensor_tensor(C2[:, n, :], C2[:, n, :], T2[:, n % 2, :], ALU.mult))
                V.tensor_tensor(B2[:, n, :], B2[:, n, :], C2[:, n, :], ALU.add).then_inc(out_ready, 1)


def slabs(w):
    k, n = w.shape
    return w.reshape(k // P, P, n // P, P).transpose(2, 1, 0, 3).reshape(n // P, P, k)


def features(v):
    v = v.reshape(-1, P)
    return v.T


def constants():
    f = np.float32
    ident = np.eye(P, dtype=f)
    ones = np.full((P, P), 1.0 / D, f)
    blk = np.kron(np.eye(2, dtype=f), np.full((HD, HD), 1.0 / HD, f))
    mats = np.stack([ident, ones, blk], 1)
    rot = np.zeros((P, P), f)
    d = np.arange(P)
    for m in range(P):
        if m % 32 < 16:
            rot[m + 16, m] = -1.0
        else:
            rot[m - 16, m] = 1.0
    i = np.arange(P)
    ahead = np.maximum(i[None, :] - i[:, None], 0)
    behind = np.maximum(i[:, None] - i[None, :], 0)
    rets = np.stack([rot, ahead, behind, np.tile(i + 1, (P, 1)), np.tile(P - i, (P, 1))], 1).astype(f)
    nf = HD // 4
    inv = f(10000.0) ** (-np.arange(nf, dtype=f) / f(nf))
    t = np.arange(SEQ)
    row, col = (t // GRID_W).astype(f), (t % GRID_W).astype(f)
    ang = np.where((d % HD < 32)[:, None], row[None, :], col[None, :]) * inv[d % nf][:, None]
    ropes = np.stack([np.cos(ang), np.sin(ang)]).astype(f)
    tab = np.zeros((4, 16), f)
    for g in range(4):
        tab[g] = 1.0 / np.minimum(np.arange(16) + 1, 2 << g)
    pooltab = np.tile(tab.reshape(1, 64), (P, 1))
    cols = np.stack([P - 1 - i, i], 1).astype(f)
    eps = np.tile(np.array([[LN_EPS, RMS_EPS]], f), (P, 1))
    return mats, rets, ropes, pooltab, cols, eps


def bias_layout(rpb):
    L, H = rpb.shape[:2]
    q = np.arange(P)
    kk = np.arange(LOC)
    out = np.empty((L, PAIRS, QT, P, 2, LOC), np.float32)
    for t in range(QT):
        k0 = min(max(t - 2, 0), QT - KEYT)
        r, c = 2 * t + q // GRID_W, q % GRID_W
        kr, kc = 2 * k0 + kk // GRID_W, kk % GRID_W
        rs = np.clip(r - WIN_H // 2, 0, ROWS - WIN_H)
        cs = np.clip(c - WIN_W // 2, 0, GRID_W - WIN_W)
        ok = ((kr[None] >= rs[:, None]) & (kr[None] < rs[:, None] + WIN_H)
              & (kc[None] >= cs[:, None]) & (kc[None] < cs[:, None] + WIN_W))
        dr = np.where(ok, kr[None] - r[:, None] + WIN_H - 1, 0)
        dc = np.where(ok, kc[None] - c[:, None] + WIN_W - 1, 0)
        part = np.where(ok[None, None], rpb[:, :, dr, dc], np.float32(MASKED))
        out[:, :, t] = part.reshape(L, PAIRS, 2, P, LOC).transpose(0, 1, 3, 2, 4)
    return out.reshape(L * PAIRS * QT, P, 2, LOC)


def kernel(**inputs):
    import concourse.bacc as _bacc
    from concourse.bass_utils import run_bass_kernel_spmd as _run

    a = {k: np.asarray(v) for k, v in inputs.items()}
    mats, rets, ropes, pooltab, cols, eps = constants()
    xall = np.concatenate([a["ctx"][0], a["x"][0]], 0)
    xT = xall.T.reshape(KD, P, T1)
    cT = np.stack([a["c"][0], a["c_ctx"]], 1).reshape(KD, P, 2).transpose(1, 0, 2).reshape(P, 2 * KD)
    modw = np.concatenate([slabs(a["w_mod"][l]) for l in range(2)])
    vals = {"cols": cols, "eps": eps}
    bm = a["b_mod"].reshape(48, P).T
    vals["bmod"] = np.stack([bm, bm], 2).reshape(P, 96)
    for l in range(2):
        vals[f"convw{l}"] = features(a["conv_w"][l])
        vals[f"convb{l}"] = features(a["conv_b"][l])
        vals[f"lng{l}"] = features(a["ln_g"][l])
        vals[f"lnb{l}"] = features(a["ln_b"][l])
        dl = a["ret_decay"][l]
        wide = np.broadcast_to(dl.reshape(1, 12), (P, 12))
        two = np.repeat(dl.reshape(2, PAIRS, 2), HD, axis=2).reshape(2 * PAIRS, P).T
        vals[f"dec{l}"] = np.concatenate([wide, two], 1)
    vals["lam"] = features(a["lru_lambda_2"][0])
    for n in ("g_mix_pre", "g_mix_post", "g_ffn_pre", "g_ffn_post", "g_ple_gate", "g_ple_post", "pool_scale"):
        vals[n] = features(a[n + "_2"][0])
    vals["rconvw"] = features(a["conv_w_2"][0])
    vals["rconvb"] = features(a["conv_b_2"][0])
    vals["b_gates"] = features(a["b_rg_gates_2"][0])
    vals["fconvw"] = features(a["ffn_conv_w_2"][0])
    vals["fconvb"] = features(a["ffn_conv_b_2"][0])
    vecs = np.concatenate([vals[n] for n in VEC], 1)
    assert vecs.shape == (P, NVEC)

    def braid(u, v):
        return np.stack([u, v], 1).reshape((-1,) + u.shape[1:])

    parts = []
    for l in range(2):
        s = slabs(a["w_in"][l])
        rk, rv, nk, nv, rq, rg, nq, ng = (s[3 * i:3 * i + 3] for i in range(8))
        ch, cb, ccg, cz = (s[24 + 2 * i:26 + 2 * i] for i in range(4))
        parts += [braid(rk, rq), braid(rv, rg), braid(nk, nv), braid(nq, ng)]
        for c in range(2):
            parts += [ccg[c:c + 1], ch[c:c + 1], cb[c:c + 1], cz[c:c + 1]]
        parts.append(slabs(a["w_out"][l]))
    s = slabs(a["w_in_2"][0])
    pool_u, rx, rg, gp, gr = s[0:4], s[4:12], s[12:20], s[20:28], s[28:36]

    up = slabs(a["w_up_2"][0])
    down = a["w_down_2"][0]
    parts += [braid(rx, rg), braid(gr, slabs(a["w_rg_out_2"][0])), pool_u, gp, slabs(a["w_o_2"][0])]
    for f in range(FF_GROUPS):
        parts += [braid(up[8 * f:8 * f + 8], up[24 + 8 * f:32 + 8 * f]), slabs(down[D * f:D * (f + 1)])]
    parts.append(slabs(a["w_ple_gate_2"][0]))
    s8 = np.concatenate(parts)
    assert s8.shape[0] == S8_END
    s4 = slabs(a["w_pool_out_2"][0])
    s2 = slabs(a["w_ple_proj_2"][0])
    wg = a["w_rg_gates_2"][0].reshape(2, 8, 2, HD, HD)
    rgw = np.zeros((2, 8, P, P), np.float32)
    rgw[:, :, :HD, :HD] = wg[:, :, 0]
    rgw[:, :, HD:, HD:] = wg[:, :, 1]
    pT = a["p_2"][0, 0].T.reshape(2, P, SEQ)
    arrays = {"xT": xT, "cT": cT, "modw": modw, "vecs": vecs, "mats": mats, "ropes": ropes, "rets": rets,
              "bias": bias_layout(a["na_rpb"]), "s8": s8, "s4": s4, "s2": s2, "rgw": rgw.reshape(16, P, P),
              "poolw": a["pool_w_2"][0], "pooltab": pooltab, "pT": pT}
    nc = _bacc.Bacc("TRN2", target_bir_lowering=False, num_devices=1)
    ins, args = {}, []
    for name, v in arrays.items():
        v = np.ascontiguousarray(v)
        ins[name] = v
        args.append(nc.dram_tensor(name, v.shape, F32, kind="ExternalInput").ap())
    args.append(nc.dram_tensor("outT", (KD, P, SEQ), F32, kind="ExternalOutput").ap())
    build_kernel(nc, *args)
    r = _run(nc, [ins], core_ids=[0])
    out = np.asarray(r.results[0]["outT"])
    return np.ascontiguousarray(out.reshape(D, SEQ).T)[None]
```
